# Optimizing a Trainium2 kernel written in Bass

```python
import jax, jax.numpy as jnp
from jax import lax
import numpy as np

D_MODEL = 1024
BATCH = 1
SEQ = 1024
DEPTH = 1
DEC_BATCH = 8
DEC_SEQ = 1
PAST_LEN = 8192
PAGE_SIZE = 128

CHUNK = 128
A_WIDTH = D_MODEL
A_HEADS = 8
A_HEAD_DIM = A_WIDTH // A_HEADS
B_WIDTH = D_MODEL
B_GROUPS = 8
CONV_W = 3
FFN_HIDDEN = ((8 * D_MODEL // 3 + 255) // 256) * 256
EPS = 1e-6
IN_COLS = 2 * A_WIDTH + 3 * B_WIDTH + 2 * D_MODEL
SPLITS = (A_WIDTH, 2 * A_WIDTH, 2 * A_WIDTH + B_WIDTH, 2 * A_WIDTH + 2 * B_WIDTH,
          2 * A_WIDTH + 3 * B_WIDTH, 2 * A_WIDTH + 3 * B_WIDTH + D_MODEL)

kernel_name = "hybrid_sgu_shortconv_decoder_step"

def rms_norm(x, g):
    xf = x.astype(jnp.float32)
    y = xf * lax.rsqrt(jnp.mean(xf * xf, axis=-1, keepdims=True) + EPS)
    return (y * g.astype(jnp.float32)).astype(x.dtype)

def layer_norm(x, g, b):
    xf = x.astype(jnp.float32)
    mu = jnp.mean(xf, axis=-1, keepdims=True)
    xc = xf - mu
    y = xc * lax.rsqrt(jnp.mean(xc * xc, axis=-1, keepdims=True) + EPS)
    return (y * g.astype(jnp.float32) + b.astype(jnp.float32)).astype(x.dtype)

def chunk_spatial_mix(v, w_s, b_s):
    nb, t, _ = v.shape
    n = -(-t // CHUNK)
    pad = n * CHUNK - t
    vp = jnp.pad(v, ((0, 0), (0, pad), (0, 0))).reshape(nb, n, CHUNK, A_HEADS, A_HEAD_DIM)
    causal = jnp.tril(jnp.ones((CHUNK, CHUNK), dtype=bool))
    ws = jnp.where(causal[None], w_s, jnp.zeros((), w_s.dtype))
    mixed = jnp.einsum("hij,bnjhd->bnihd", ws, vp) + b_s.T[:, :, None]
    return mixed.reshape(nb, n * CHUNK, A_WIDTH)[:, :t]

def short_conv(xp, w):
    t = xp.shape[1] - (CONV_W - 1)
    out = xp[:, 0:t] * w[0]
    for k in range(1, CONV_W):
        out = out + xp[:, k:k + t] * w[k]
    return out

def hybrid_mixer(xn, conv_hist, w_in, sgu_ln_g, sgu_ln_b, w_s, b_s, conv_w, w_a_out, w_b_out, w_o):
    z = jnp.einsum("btd,dc->btc", xn, w_in)
    u, v, b_gate, c_gate, x_in, r_a, r_b = jnp.split(z, SPLITS, axis=-1)
    u = jax.nn.gelu(u)
    v = layer_norm(jax.nn.gelu(v), sgu_ln_g, sgu_ln_b)
    y_a = jnp.einsum("btc,cd->btd", u * chunk_spatial_mix(v, w_s, b_s), w_a_out)
    c_in = c_gate * x_in
    xp = jnp.concatenate([conv_hist.astype(c_in.dtype), c_in], axis=1)
    y_b = jnp.einsum("btc,cd->btd", b_gate * short_conv(xp, conv_w), w_b_out)
    h = jax.nn.sigmoid(r_a) * y_a + jax.nn.sigmoid(r_b) * y_b
    out = jnp.einsum("btd,de->bte", h, w_o)
    return out, xp[:, -(CONV_W - 1):], v

def swiglu(x, w_gate, w_up, w_down):
    g = jnp.einsum("btd,df->btf", x, w_gate)
    up = jnp.einsum("btd,df->btf", x, w_up)
    return jnp.einsum("btf,fd->btd", jax.nn.silu(g) * up, w_down)

def decoder_layer(x, conv_hist, mix_pre_g, mix_post_g, w_in, sgu_ln_g, sgu_ln_b, w_s, b_s, conv_w,
                  w_a_out, w_b_out, w_o, ffn_pre_g, ffn_post_g, w_gate, w_up, w_down):
    h, new_hist, v = hybrid_mixer(rms_norm(x, mix_pre_g), conv_hist, w_in, sgu_ln_g, sgu_ln_b,
                                  w_s, b_s, conv_w, w_a_out, w_b_out, w_o)
    x = x + rms_norm(h, mix_post_g)
    f = swiglu(rms_norm(x, ffn_pre_g), w_gate, w_up, w_down)
    x = x + rms_norm(f, ffn_post_g)
    return x, new_hist, v

def setup_inputs(seed: int = 0) -> dict:
    key = jax.random.key(seed)
    ks = jax.random.split(key, 24)
    f32 = jnp.float32
    nrm = lambda k, shape, s: (jax.random.normal(k, shape, f32) * s)
    gain = lambda k, shape: (1.0 + 0.05 * jax.random.normal(k, shape, f32))
    return {
        "x_prompt": nrm(ks[0], (BATCH, SEQ, D_MODEL), 1.0),
        "x_sample": nrm(ks[1], (DEC_BATCH, DEC_SEQ, D_MODEL), 1.0),
        "state_conv": nrm(ks[2], (DEPTH, DEC_BATCH, CONV_W - 1, B_WIDTH), 0.5),
        "mix_pre_g": gain(ks[3], (DEPTH, D_MODEL)),
        "mix_post_g": gain(ks[4], (DEPTH, D_MODEL)),
        "w_in": nrm(ks[5], (DEPTH, D_MODEL, IN_COLS), D_MODEL ** -0.5),
        "sgu_ln_g": gain(ks[6], (DEPTH, A_WIDTH)),
        "sgu_ln_b": nrm(ks[7], (DEPTH, A_WIDTH), 0.02),
        "w_s": nrm(ks[8], (DEPTH, A_HEADS, CHUNK, CHUNK), CHUNK ** -0.5),
        "b_s": 1.0 + nrm(ks[9], (DEPTH, A_HEADS, CHUNK), 0.1),
        "conv_w": nrm(ks[10], (DEPTH, CONV_W, B_WIDTH), CONV_W ** -0.5),
        "w_a_out": nrm(ks[11], (DEPTH, A_WIDTH, D_MODEL), A_WIDTH ** -0.5),
        "w_b_out": nrm(ks[12], (DEPTH, B_WIDTH, D_MODEL), B_WIDTH ** -0.5),
        "w_o": nrm(ks[13], (DEPTH, D_MODEL, D_MODEL), D_MODEL ** -0.5),
        "ffn_pre_g": gain(ks[14], (DEPTH, D_MODEL)),
        "ffn_post_g": gain(ks[15], (DEPTH, D_MODEL)),
        "w_gate": nrm(ks[16], (DEPTH, D_MODEL, FFN_HIDDEN), D_MODEL ** -0.5),
        "w_up": nrm(ks[17], (DEPTH, D_MODEL, FFN_HIDDEN), D_MODEL ** -0.5),
        "w_down": nrm(ks[18], (DEPTH, FFN_HIDDEN, D_MODEL), FFN_HIDDEN ** -0.5),
    }

def reference(x_prompt, x_sample, state_conv, mix_pre_g, mix_post_g, w_in, sgu_ln_g, sgu_ln_b, w_s,
              b_s, conv_w, w_a_out, w_b_out, w_o, ffn_pre_g, ffn_post_g, w_gate, w_up, w_down):
    xp_ = x_prompt
    xs_ = x_sample
    conv_prompt, conv_sample, chunk_v_sample = [], [], []
    for l in range(DEPTH):
        params = (mix_pre_g[l], mix_post_g[l], w_in[l], sgu_ln_g[l], sgu_ln_b[l], w_s[l], b_s[l],
                  conv_w[l], w_a_out[l], w_b_out[l], w_o[l], ffn_pre_g[l], ffn_post_g[l],
                  w_gate[l], w_up[l], w_down[l])
        hist0 = jnp.zeros((xp_.shape[0], CONV_W - 1, B_WIDTH), xp_.dtype)
        xp_, hp, _ = decoder_layer(xp_, hist0, *params)
        xs_, hs, vs = decoder_layer(xs_, state_conv[l], *params)
        conv_prompt.append(hp)
        conv_sample.append(hs)
        chunk_v_sample.append(vs)
    new_conv_prompt = jnp.stack(conv_prompt)
    new_conv_sample = jnp.stack(conv_sample)
    new_chunk_v_sample = jnp.stack(chunk_v_sample)
    return (xp_, xs_, new_conv_prompt, new_conv_sample, new_chunk_v_sample)


_drawn_inputs = setup_inputs


def setup_inputs(seed=0):
    import zlib

    import numpy as np

    out = dict(_drawn_inputs(seed))
    spreads = {}
    factors = {'sgu_ln_b': 2.875}
    for name, (base, spread) in spreads.items():
        noise = np.random.default_rng([zlib.crc32(name.encode()), seed]).standard_normal(out[name].shape)
        drawn = base * np.exp(spread * noise) if base else spread * noise
        out[name] = __import__('jax').numpy.asarray(drawn.astype(out[name].dtype))
    for name, factor in factors.items():
        out[name] = (out[name] * factor).astype(out[name].dtype)
    return out
```

```python
from contextlib import ExitStack

import numpy as np

import concourse.bass as bass
from concourse import mybir

D = 1024
SEQ = 1024
NS = 8
TOK = NS + SEQ
KT = D // 128
CH = 3
CW = TOK // CH
FFN = 2816
EPS = 1e-6
PAIRS = FFN // 256
COL_U, COL_V, COL_B, COL_C, COL_X, COL_RA, COL_RB = (i * D for i in range(7))

R_U = 0
R_A = R_U + KT
R_C = R_A + 2 * KT
R_B = R_C + 3 * KT
R_O = R_B + 2 * KT
R_F = R_O + CH * KT
R_LOOP = R_F + 4
R_END = R_F + 6 * PAIRS
FREE = 9

START = 1

P_POST, P_PRE, P_CONV, P_ROWS = 0, KT, 2 * KT, 5 * KT


def build(nc, x_prompt, x_sample, state_conv, mix_pre_g, mix_post_g, w_in, sgu_ln_g, sgu_ln_b, w_s,
          b_s, conv_w, w_a_out, w_b_out, w_o, ffn_pre_g, ffn_post_g, w_gate, w_up, w_down,
          y_prompt, y_sample, conv_prompt, conv_sample, v_sample):
    f32, f32r, i32 = mybir.dt.float32, mybir.dt.float32r, mybir.dt.int32
    ALU, ACT = mybir.AluOpType, mybir.ActivationFunctionType
    MUL, ADD, SUB = ALU.mult, ALU.add, ALU.subtract
    ds = bass.ds

    xt_dram = nc.dram_tensor("xt_dram", [128, KT, TOK], f32, kind="Internal").ap()

    ctx = ExitStack()
    with ctx:
        def sb(name, shape, dt=f32):
            return ctx.enter_context(nc.sbuf_tensor(name, shape, dt))

        def sem(name):
            return ctx.enter_context(nc.semaphore(name))

        xn_hi = sb("xn_hi", [128, KT, TOK], f32r)
        xn_lo = sb("xn_lo", [128, KT, TOK], f32r)
        tile_bytes = KT * TOK * 4
        op_at = (nc.sbuf_usable_end - 2 * tile_bytes) // 32 * 32
        op_hi = nc.alloc_sbuf_tensor_at("op_hi", [128, KT, TOK], f32r, offset=op_at)
        op_lo = nc.alloc_sbuf_tensor_at("op_lo", [128, KT, TOK], f32r, offset=op_at + tile_bytes)
        xt = nc.alloc_sbuf_tensor_at("xt", [128, KT, TOK], f32, offset=op_at)
        hid = op_lo
        g = sb("g", [128, KT, TOK])
        gv = g[:, :, 0:D]
        stage = [sb(f"stage{i}", [128, D]) for i in range(2)]
        ring_hi = [sb(f"ring_hi{i}", [128, D], f32r) for i in range(2)]
        ring_lo = [sb(f"ring_lo{i}", [128, D], f32r) for i in range(2)]
        tmp = [sb(f"tmp{i}", [128, TOK + 2]) for i in range(8)]
        ident = sb("ident", [128, 128])
        ones = sb("ones", [128, 128])
        par_rows = sb("par_rows", [P_ROWS, 128])
        par = sb("par", [128, P_ROWS])
        hist = sb("hist", [128, KT, 2, NS])
        ws00 = sb("ws00", [128, KT])
        mix_s = sb("mix_s", [128, KT, NS])
        tail = sb("tail", [128, 2 + NS, KT])
        tail_out = sb("tail_out", [(2 + NS) * KT, 128])
        small = sb("small", [128, 64])
        assert nc.sbuf_base <= op_at, (nc.sbuf_base, op_at)
        eps = small[:, 60:61]
        warm = small[:, 61:62]
        ps = ctx.enter_context(nc.psum_tensor("ps", [128, 8, 512], f32))

        x_rows = [tmp[0], tmp[1]]
        x_norm, x_save, pre_gain, v_smp, ws_t, ws_rows = tmp[2:8]
        hist_rows = tmp[5]
        act_out, v_head, prod, ln_g, ln_b = tmp[0:5]
        b_rows = tmp[7]
        c_in = tmp[1]

        def group(i):
            return ps[:, 3 * i:3 * i + 3, 0:CW]

        def chunks(ap):
            return ap.rearrange("p (c w) -> p c w", c=CH)

        def flat2(t, m):
            return t[:, ds(m, 1), :].rearrange("p a n -> p (a n)")

        def flat3(t, m):
            return t[:, ds(m, 1), :].rearrange("p a (c w) -> p (a c) w", c=CH)

        def bank_pair(b, n=128):
            return ps[:, b:b + 2, :].rearrange("p a (k c) -> p (a k) c", c=128)[:, :, 0:n]

        def tokens(t):
            return (128, NS + 128 * t) if t < 8 else (NS, 0)

        consts = sem("consts")
        x_in = [sem("x_in0"), sem("x_in1")]
        wv_in = [sem(f"wv_in{k}") for k in range(KT)]
        wv_hi, wv_lo = sem("wv_hi"), sem("wv_lo")
        pre_in, ws_in, row_in, ws00_in = sem("pre_in"), sem("ws_in"), sem("row_in"), sem("ws00_in")
        ws_masked = sem("ws_masked")
        sumsq, x_scaled = sem("sumsq"), sem("x_scaled")
        raw_turned, norm_turned = sem("raw_turned"), sem("norm_turned")
        raw_copied, xt_saved = sem("raw_copied"), sem("xt_saved")
        xn_hi_done, xn_lo_done = sem("xn_hi_done"), sem("xn_lo_done")
        v_gelu, v_norm = sem("v_gelu"), sem("v_norm")
        chain = sem("chain")
        const_turned, ws_copied, par_copied = sem("const_turned"), sem("ws_copied"), sem("par_copied")
        ln_g_in, ln_b_in, b_in = sem("ln_g_in"), sem("ln_b_in"), sem("b_in")
        vs_ready, vs_turned, vs_out, mix_s_ready = sem("vs_ready"), sem("vs_turned"), sem("vs_out"), sem("mix_s_ready")
        w_in_done = [sem("w_loaded0"), sem("w_loaded1")]
        w_hi, pool_hi, w_lo = sem("w_hi"), sem("pool_hi"), sem("w_lo")
        acc_full = sem("acc_full")
        u_gelu, head_scaled, head_ready = sem("u_gelu"), sem("head_scaled"), sem("head_ready")
        mixed, mix_biased, u_prod = sem("mixed"), sem("mix_biased"), sem("u_prod")
        op_hi_done, op_lo_done = sem("op_hi_done"), sem("op_lo_done")
        a_sig, a_out = sem("a_sig"), sem("a_out")
        c_copied, cx_done, conv_step, h_conv, c_prod = sem("c_copied"), sem("cx_done"), sem("conv_step"), sem("h_conv"), sem("c_prod")
        tail_turned, tail_copied, tail_saved, hist_saved = sem("tail_turned"), sem("tail_copied"), sem("tail_saved"), sem("hist_saved")
        b_sig, b_out, h_sum = sem("b_sig"), sem("b_out"), sem("h_sum")
        h_hi, h_lo = sem("h_hi"), sem("h_lo")
        xt_in = sem("xt_in")
        o_copied, o_sq, o_acc = sem("o_copied"), sem("o_sq"), sem("o_acc")
        n_sum, n_sqrt, n_base, n_step = sem("n_sum"), sem("n_sqrt"), sem("n_base"), sem("n_step")
        x1_done, x1_sq, x1_total, x1n_ready, x1n_hi, x1n_lo = sem("x1_done"), sem("x1_sq"), sem("x1_total"), sem("x1n_ready"), sem("x1n_hi"), sem("x1n_lo")
        f_silu, f_prod, hid_hi, hid_lo, f_acc = sem("f_silu"), sem("f_prod"), sem("hid_hi"), sem("hid_lo"), sem("f_acc")
        post_in, y_turned, y_sumsq, y_scaled, y_ready = sem("post_in"), sem("y_turned"), sem("y_sumsq"), sem("y_scaled"), sem("y_ready")
        y_out = [sem("y_out0"), sem("y_out1")]

        def base(j):
            return FREE + R_LOOP + 12 * (j - 1)

        block = ctx.enter_context(nc.Block())

        @block.sync
        def _(sp):
            def x_load(t):
                rows, _ = tokens(t)
                if t >= 2:
                    sp.wait_ge(raw_turned, t - 1)
                    sp.wait_ge(x_scaled, t - 1)
                src = x_prompt[0, 128 * t:128 * t + 128, :] if t < 8 else x_sample[:, 0, :]
                sp.dma_start(x_rows[t % 2][0:rows, 0:D], src).then_inc(x_in[t % 2], 16)

            def wv_load(k):
                sp.dma_start(gv[:, k, :], w_in[0, 128 * k:128 * k + 128, COL_V:COL_V + D]).then_inc(wv_in[k], 16)

            def load(slot, src):
                sp.dma_start(stage[slot][:, :].rearrange("p (k c) -> p k c", k=src.shape[1]), src) \
                    .then_inc(w_in_done[slot], 16)

            def columns(w, at):
                return w.rearrange("(k p) n -> p k n", p=128)[:, :, ds(at, 128)]

            def down(j, half):
                return w_down[0].rearrange("(j k p) n -> p j k n", p=128, k=2)[:, ds(j, 1), :, 512 * half:512 * half + 512] \
                    .rearrange("p a k n -> p (a k) n")

            x_load(0)
            wv_load(0)
            wv_load(1)
            wv_load(2)
            x_load(1)
            for k in range(3, KT):
                wv_load(k)
            load(0, columns(w_in[0], COL_U))
            load(1, columns(w_in[0], COL_U + 128))
            for t in range(2, 9):
                x_load(t)
            sp.wait_ge(x_scaled, 9)
            sp.dma_start(ln_b[:, 0:D], sgu_ln_b[0:1, :].to_broadcast((128, D))).then_inc(ln_b_in, 16)
            sp.wait_ge(xt_saved, 16 * 9)
            sp.dma_start(ln_g[:, 0:D], sgu_ln_g[0:1, :].to_broadcast((128, D))).then_inc(ln_g_in, 16)
            sp.wait_ge(const_turned, 1)
            sp.dma_start(b_rows[:, 0:D], b_s[0:1].rearrange("a h i -> a (h i)").to_broadcast((128, D))).then_inc(b_in, 16)

            for m in range(2, KT):
                sp.wait_ge(w_lo, R_U + m - 1)
                load(m % 2, columns(w_in[0], COL_U + m * 128))
            with sp.Fori(1, KT + 1) as n:
                for s, (w, c0) in enumerate(((w_in[0], COL_RA), (w_a_out[0], 0))):
                    sp.wait_ge(w_lo, R_A + 2 * n - 2 + s - 1)
                    load(s, columns(w, n * 128 + c0 - 128))
            with sp.Fori(0, KT // 2) as i:
                for n in range(6):
                    at = sp.snap((COL_C, COL_X, COL_B)[n % 3] + n // 3 * 128 + i * 256)
                    sp.wait_ge(w_lo, R_C + 6 * i + n - 1)
                    load(n % 2, columns(w_in[0], at))
            with sp.Fori(1, KT + 1) as n:
                for s, (w, c0) in enumerate(((w_in[0], COL_RB), (w_b_out[0], 0))):
                    sp.wait_ge(w_lo, R_B + 2 * n - 2 + s - 1)
                    load(s, columns(w, n * 128 + c0 - 128))
            for s in range(2):
                sp.wait_ge(w_lo, R_O + s - 1)
                load(s, columns(w_o[0], s * 128))
            sp.wait_ge(acc_full, FREE + R_O)
            sp.dma_start(xt[:, :, :], xt_dram).then_inc(xt_in, 16)
            for n in range(2, CH * KT):
                sp.wait_ge(w_lo, R_O + n - 1)
                load(n % 2, columns(w_o[0], n % KT * 128))
            for n in range(8):
                sp.wait_ge(w_lo, R_F + n - 1)
                load(n % 2, columns((w_gate, w_up)[n % 2][0], n // 2 * 128))
            with sp.Fori(1, PAIRS - 1) as j:
                for n in range(2):
                    pair = sp.snap(j - 1)
                    sp.wait_ge(w_lo, R_LOOP + 6 * j - 2 + n - 1)
                    load(n, down(pair, n))
                for n in range(4):
                    at = sp.snap(j * 256 + 256 + n // 2 * 128)
                    sp.wait_ge(w_lo, R_LOOP + 6 * j + n - 1)
                    load(n % 2, columns((w_gate, w_up)[n % 2][0], at))
            for n in range(4):
                sp.wait_ge(w_lo, R_LOOP + 6 * (PAIRS - 1) - 2 + n - 1)
                load(n % 2, down(PAIRS - 2 + n // 2, n % 2))
            sp.dma_start(tmp[7][:, 0:D], ffn_post_g[0:1, :].to_broadcast((128, D))).then_inc(post_in, 16)

            for t in range(9):
                rows, _ = tokens(t)
                sp.wait_ge(y_ready, t + 1)
                dst = y_prompt[0, 128 * t:128 * t + 128, :] if t < 8 else y_sample[:, 0, :]
                sp.dma_start(dst, tmp[5 + t % 2][0:rows, 0:D]).then_inc(y_out[t % 2], 16)
            sp.wait_ge(y_out[0], 16 * 5)
            sp.wait_ge(y_out[1], 16 * 4)
            sp.wait_ge(vs_out, 16)
            sp.wait_ge(hist_saved, 16)
            sp.wait_ge(tail_saved, 16 * (1 + NS))
            sp.wait_ge(xt_saved, 16 * 9)

        @block.gpsimd
        def _(pool):
            pool.memset(ident[:, :], 0.0).then_inc(consts, 1)
            pool.memset(ones[:, :], 1.0).then_inc(consts, 1)
            pool.memset(eps, EPS).then_inc(consts, 1)
            pool.wait_ge(consts, 3)
            pool.affine_select(out=ident[:, :], in_=ident[:, :], compare_op=ALU.not_equal, fill=1.0, base=0,
                               pattern=[[-1, 128]], channel_multiplier=1).then_inc(consts, 1)
            pool.wait_ge(ws_in, 16)
            wsv = ws_rows[:, 0:D].rearrange("p (h j) -> p h j", h=KT)
            pool.affine_select(out=wsv, in_=wsv, compare_op=ALU.is_ge, fill=0.0, base=0,
                               pattern=[[0, KT], [-1, 128]], channel_multiplier=1).then_inc(ws_masked, 1)

            def rest(s):
                pool.tensor_tensor(ring_lo[s][:, :], stage[s][:, :], ring_hi[s][:, :].bitcast(f32), SUB) \
                    .then_inc(w_lo, 1)

            def split(r, count):
                pool.wait_ge(w_in_done[r % 2], 16 * (r // 2 + 1))
                pool.wait_ge(acc_full, FREE + r - 1)
                pool.tensor_copy(ring_hi[r % 2][:, :], stage[r % 2][:, :]).then_inc(pool_hi, 1)
                pool.wait_ge(pool_hi, count)
                rest(r % 2)

            split(0, 1)
            split(1, 2)
            with pool.Fori(1, R_O // 2) as i:
                for s in range(2):
                    pool.wait_ge(w_hi, 2 * i + s - 1)
                    rest(s)
            for r in range(R_O, R_F + 2):
                split(r, r - R_O + 3)
            with pool.Fori(R_F // 2 + 1, R_END // 2) as i:
                for s in range(2):
                    pool.wait_ge(w_hi, 2 * i + s - 1 - (R_F + 2 - R_O))
                    rest(s)

        @block.tensor
        def _(pe):
            def three(out, w_h, w_l, x_h, x_l, first, last):
                ins = None
                for n, (w, x) in enumerate(((w_h, x_h), (w_h, x_l), (w_l, x_h))):
                    for o, xc in zip(out, x):
                        ins = pe.matmul(o, w, xc, start=first and n == 0, stop=last and n == 2)
                return ins

            def parts(x, k, n=CH):
                return [x[:, k, CW * c:CW * c + CW] for c in range(n)]

            def unit(slot, grp, x_h, x_l):
                out = [ps[:, 3 * grp + c, 0:CW] for c in range(CH)]
                for k in range(KT):
                    w = slice(128 * k, 128 * k + 128)
                    ins = three(out, ring_hi[slot][:, w], ring_lo[slot][:, w], parts(x_h, k), parts(x_l, k), k == 0, k == KT - 1)
                ins.then_inc(acc_full, 1)

            def turn(t):
                rows, _ = tokens(t)
                pe.wait_ge(x_in[t % 2], 16 * (t // 2 + 1))
                if t:
                    pe.wait_ge(raw_copied, t)
                for k in range(KT):
                    ins = pe.transpose(ps[:, 4 + k // 4, 128 * (k % 4):128 * (k % 4) + rows],
                                       x_rows[t % 2][0:rows, 128 * k:128 * k + 128], ident[0:rows, 0:rows])
                ins.then_inc(raw_turned, 1)
                pe.wait_ge(x_scaled, t + 1)
                if t:
                    pe.wait_ge(xn_lo_done, t)
                for k in range(KT):
                    ins = pe.transpose(ps[:, 6 + k // 4, 128 * (k % 4):128 * (k % 4) + rows],
                                       x_norm[0:rows, 128 * k:128 * k + 128], ident[0:rows, 0:rows])
                ins.then_inc(norm_turned, 1)

            def v_tile(t):
                _, at = tokens(t)
                pe.wait_ge(xn_lo_done, t + 1)
                if t >= 2:
                    pe.wait_ge(v_gelu, t - 1)
                out = [ps[:, 2 * (t % 2) + n, :] for n in range(2)]
                for k in range(KT):
                    if t == 0:
                        pe.wait_ge(wv_lo, k + 1)
                    w_h, w_l = ([w[:, k, 512 * n:512 * n + 512] for n in range(2)] for w in (op_hi, op_lo))
                    ins = three(out, xn_hi[:, k, at:at + 128], xn_lo[:, k, at:at + 128], w_h, w_l, k == 0, k == KT - 1)
                ins.then_inc(acc_full, 1)

            pe.sem_inc(mixed, START)
            pe.wait_ge(consts, 4)
            turn(0)
            turn(1)
            for t in range(9):
                v_tile(t)
                if t + 2 < 9:
                    turn(t + 2)
                if t == 7:
                    pe.wait_ge(raw_copied, 9)
                    pe.wait_ge(xn_lo_done, 9)
                    pe.wait_ge(row_in, 16 * 5)
                    pe.wait_ge(ws_masked, 1)
                    pe.transpose(ps[:, 4, 0:P_ROWS], par_rows[:, :], ident[0:P_ROWS, 0:P_ROWS])
                    for k in range(KT):
                        pe.transpose(ps[:, 4, 128 + 16 * k:144 + 16 * k], hist_rows[0:2 * NS, 128 * k:128 * k + 128],
                                     ident[0:2 * NS, 0:2 * NS])
                    for h in range(KT):
                        ins = pe.transpose(ps[:, 6 + h // 4, 128 * (h % 4):128 * (h % 4) + 128],
                                           ws_rows[:, 128 * h:128 * h + 128], ident[:, :])
                    ins.then_inc(const_turned, 1)
            pe.wait_ge(v_gelu, 9)
            pe.wait_ge(par_copied, 1)

            def mix(m):
                pe.wait_ge(head_ready, m + 1)
                pe.wait_ge(mix_biased, m)
                for n in range(8):
                    ins = pe.matmul(ps[:, 6 + n // 4, 128 * (n % 4):128 * (n % 4) + 128],
                                    v_head[:, 128 * n:128 * n + 128], ws_t[:, ds(m * 128, 128)], start=True, stop=True)
                ins.then_inc(mixed, 1)

            pe.wait_ge(w_lo, 1)
            unit(0, 0, xn_hi, xn_lo)
            pe.wait_ge(vs_ready, 1)
            pe.wait_ge(ws_copied, 1)
            for k in range(KT):
                ins = pe.transpose(ps[:, 7, NS * k:NS * k + NS], v_smp[0:NS, 128 * k:128 * k + 128], ident[0:NS, 0:NS])
            ins.then_inc(vs_turned, 1)
            pe.wait_ge(mix_s_ready, 1)
            mix(0)
            pe.wait_ge(w_lo, 2)
            unit(1, 1, xn_hi, xn_lo)
            mix(1)
            with nc.Fori(1, KT // 2, engines=[mybir.EngineType.PE], hint_back_edge=True) as i:
                for s in range(2):
                    m = 2 * i + s
                    pe.wait_ge(w_lo, R_U + m + 1)
                    pe.wait_ge(u_gelu, m - 1)
                    unit(s, s, xn_hi, xn_lo)
                    mix(m)

            pe.wait_ge(u_gelu, KT)
            with nc.Fori(0, KT, engines=[mybir.EngineType.PE], hint_back_edge=True) as m:
                pe.wait_ge(w_lo, R_A + 2 * m + 1)
                pe.wait_ge(a_sig, START + m)
                unit(0, 0, xn_hi, xn_lo)
                pe.wait_ge(w_lo, R_A + 2 * m + 2)
                pe.wait_ge(a_out, START + m)
                pe.wait_ge(op_lo_done, START + KT)
                unit(1, 1, op_hi, op_lo)

            with nc.Fori(0, KT // 2, engines=[mybir.EngineType.PE], hint_back_edge=True) as i:
                for n in range(6):
                    m = 2 * i + n // 3
                    pe.wait_ge(w_lo, R_C + 6 * i + n + 1)
                    if n % 3 == 0:
                        pe.wait_ge(cx_done, START + m)
                        if n == 0:
                            pe.wait_ge(a_sig, START + KT)
                    elif n % 3 == 1:
                        pe.wait_ge(c_prod, START + m)
                        if n == 1:
                            pe.wait_ge(a_out, START + KT)
                    else:
                        pe.wait_ge(c_copied, m + 1)
                    unit(n % 2, n % 2, xn_hi, xn_lo)

            pe.wait_ge(cx_done, START + KT)
            pe.wait_ge(c_prod, START + KT)
            pe.transpose(ps[0:(2 + NS) * KT, 6, 0:128], tail[:, :, :].rearrange("p j m -> p (j m)"), ident[:, :]) \
                .then_inc(tail_turned, 1)
            with nc.Fori(0, KT, engines=[mybir.EngineType.PE], hint_back_edge=True) as m:
                pe.wait_ge(w_lo, R_B + 2 * m + 1)
                pe.wait_ge(b_sig, START + m)
                unit(0, 0, xn_hi, xn_lo)
                pe.wait_ge(w_lo, R_B + 2 * m + 2)
                pe.wait_ge(b_out, START + m)
                pe.wait_ge(op_lo_done, START + 2 * KT)
                unit(1, 1, op_hi, op_lo)

            def norm_sum(n, at):
                pe.matmul(ps[:, 6 + n % 2, 0:CW], ones[:, :], at, start=True, stop=True).then_inc(n_sum, 1)

            def first_norm(c):
                pe.wait_ge(o_acc, KT * (c + 1))
                norm_sum(0, tmp[3][:, 0:CW])

            def second_norm(c):
                pe.wait_ge(x1_total, c + 1)
                norm_sum(1, tmp[4][:, 0:CW])

            pe.wait_ge(b_sig, START + KT)
            pe.wait_ge(b_out, START + KT)
            pe.wait_ge(h_lo, KT)
            pe.wait_ge(tail_copied, 1)
            for c in range(CH):
                for m in range(KT):
                    n = KT * c + m
                    pe.wait_ge(w_lo, R_O + n + 1)
                    if n >= 6:
                        pe.wait_ge(o_copied, n - 5)
                    for k in range(KT):
                        w = slice(128 * k, 128 * k + 128)
                        t = slice(CW * c, CW * c + CW)
                        ins = three([ps[:, n % 6, 0:CW]], ring_hi[n % 2][:, w], ring_lo[n % 2][:, w],
                                    [xn_hi[:, k, t]], [xn_lo[:, k, t]], k == 0, k == KT - 1)
                    ins.then_inc(acc_full, 1)
                    if c and m == 0:
                        first_norm(c - 1)
                    if c and m == 5:
                        second_norm(c - 1)
            first_norm(CH - 1)
            second_norm(CH - 1)

            pe.wait_ge(x1n_lo, CH)
            pe.wait_ge(o_copied, CH * KT)
            for n in range(4):
                pe.wait_ge(w_lo, R_F + n + 1)
                if n == 2:
                    pe.wait_ge(f_silu, 1)
                if n == 3:
                    pe.wait_ge(f_prod, 1)
                unit(n % 2, n % 2, xn_hi, xn_lo)

            def down(j, gates):
                pe.wait_ge(hid_lo, 2 * j)
                for m in range(KT):
                    slot = m // 4
                    if m % 4 == 0:
                        pe.wait_ge(w_lo, R_LOOP + 6 * (j - 1) + gates + slot + 1)
                    if m < 2 and gates:
                        pe.wait_ge((f_silu, f_prod)[m], 2 * j + 2)
                    else:
                        pe.wait_ge(f_acc, START + 8 * j - 8 + m)
                    for k in range(2):
                        w = slice(512 * k + 128 * (m % 4), 512 * k + 128 * (m % 4) + 128)
                        at = ((j - 1) % 2) * 2 + k
                        x_h, x_l = ([hid[:, ds(o + at, 1), CW * c:CW * c + CW].rearrange("p a n -> p (a n)") for c in range(CH)]
                                    for o in (0, 4))
                        ins = three([ps[:, 3 * (m % 2) + c, 0:CW] for c in range(CH)],
                                    ring_hi[slot][:, w], ring_lo[slot][:, w], x_h, x_l, k == 0, k == 1)
                    ins.then_inc(acc_full, 1)

            with nc.Fori(1, PAIRS, engines=[mybir.EngineType.PE], hint_back_edge=True) as j:
                for n in range(4):
                    pe.wait_ge(w_lo, R_LOOP + 6 * (j - 1) + n + 1)
                    if n < 2:
                        pe.wait_ge(f_acc, START + 8 * j - 8 + n)
                    pe.wait_ge((f_silu, f_prod)[n % 2], 2 * j + n // 2)
                    unit(n % 2, n % 2, xn_hi, xn_lo)
                down(j, 4)
            down(PAIRS, 0)

            pe.wait_ge(f_acc, START + 1 + 8 * PAIRS)
            for t in range(9):
                _, at = tokens(t)
                if t >= 2:
                    pe.wait_ge(y_ready, t - 1)
                for b, src in ((2 * (t % 2), g), (4 + 2 * (t % 2), xt)):
                    for k in range(KT):
                        ins = pe.transpose(ps[:, b + k // 4, 128 * (k % 4):128 * (k % 4) + 128],
                                           src[:, k, at:at + 128], ident[:, :])
                ins.then_inc(y_turned, 1)

        @block.scalar
        def _(act):
            act.dma_start(pre_gain[:, 0:D], mix_pre_g[0:1, :].to_broadcast((128, D))).then_inc(pre_in, 16)
            for n, src in enumerate((mix_post_g, ffn_pre_g)):
                act.dma_start(par_rows[KT * n:KT * n + KT, :], src[0].rearrange("(k p) -> k p", p=128)).then_inc(row_in, 16)
            act.dma_start(par_rows[P_CONV:P_ROWS, :], conv_w[0].rearrange("w (k p) -> (w k) p", p=128)).then_inc(row_in, 16)
            for n in range(2):
                act.dma_start(hist_rows[NS * n:NS * n + NS, 0:D], state_conv[0, :, n, :]).then_inc(row_in, 16)
            act.dma_start(ws_rows[:, 0:D].rearrange("p (h j) -> p h j", h=KT), w_s[0].rearrange("h i j -> i h j")).then_inc(ws_in, 16)
            with nc.allow_non_contiguous_dma(reason="8 scalars to each partition"):
                act.dma_start(ws00[:, :], w_s[0, :, 0, 0:1].rearrange("h a -> a h").to_broadcast((128, KT))).then_inc(ws00_in, 16)
            act.dma_start(conv_sample[0, :, 0, :], state_conv[0, :, 1, :]).then_inc(hist_saved, 16)
            for counted in (a_sig, b_sig):
                act.sem_inc(counted, START)
            act.wait_ge(consts, 3)
            act.activation(warm, eps, ACT.Gelu_apprx_tanh)

            def square(t):
                rows, _ = tokens(t)
                act.wait_ge(x_in[t % 2], 16 * (t // 2 + 1))
                if t:
                    act.wait_ge(norm_turned, t)
                act.activation(x_norm[0:rows, 0:D], x_rows[t % 2][0:rows, 0:D], ACT.Square,
                               accum_out=small[0:rows, t:t + 1]).then_inc(sumsq, 1)

            def wv_split(k):
                act.wait_ge(wv_in[k], 16)
                act.activation(op_hi[:, k, 0:D], gv[:, k, :], ACT.Copy).then_inc(wv_hi, 1)

            def keep(t):
                rows, at = tokens(t)
                act.wait_ge(raw_turned, t + 1)
                if t:
                    act.wait_ge(xt_saved, 16 * t)
                saved = x_save[:, 0:KT * rows].rearrange("p (k n) -> p k n", k=KT)
                act.activation(saved, bank_pair(4, rows), ACT.Copy).then_inc(raw_copied, 1)
                act.wait_ge(norm_turned, t + 1)
                act.activation(xn_hi[:, :, at:at + rows], bank_pair(6, rows), ACT.Copy).then_inc(xn_hi_done, 1)
                act.wait_ge(raw_copied, t + 1)
                act.dma_start(xt_dram[:, :, at:at + rows], saved).then_inc(xt_saved, 16)

            square(0)
            for k in range(3):
                wv_split(k)
            keep(0)
            square(1)
            for k in range(3, KT):
                wv_split(k)
            keep(1)
            for t in range(9):
                if t + 2 < 9:
                    square(t + 2)
                act.wait_ge(acc_full, t + 1)
                rows, _ = tokens(t)
                if t < 8:
                    if t == 0:
                        act.wait_ge(wv_lo, KT)
                    dst = gv[:, t, :]
                else:
                    act.wait_ge(const_turned, 1)
                    dst = v_smp[0:NS, 0:D]
                act.activation(dst.rearrange("p (a n) -> p a n", a=2), ps[0:rows, 2 * (t % 2):2 * (t % 2) + 2, :],
                               ACT.Gelu_apprx_tanh).then_inc(v_gelu, 1)
                if t + 2 < 9:
                    keep(t + 2)
            act.wait_ge(const_turned, 1)
            act.activation(ws_t[:, 0:D].rearrange("p (k n) -> p k n", k=KT), bank_pair(6), ACT.Copy).then_inc(ws_copied, 1)

            def ring_split(s, loads):
                act.wait_ge(w_in_done[s], 16 * loads)
                act.activation(ring_hi[s][:, :], stage[s][:, :], ACT.Copy).then_inc(w_hi, 1)

            def op_split(m, n):
                act.activation(flat2(op_hi, m), prod[:, 0:TOK], ACT.Copy).then_inc(op_hi_done, 1)

            with act.Fori(0, KT // 2) as i:
                for s in range(2):
                    m = 2 * i + s
                    act.wait_ge(acc_full, FREE + R_U + m + 1)
                    act.wait_ge(u_prod, START + m)
                    act.activation(chunks(act_out[:, 0:TOK]), group(s), ACT.Gelu_apprx_tanh).then_inc(u_gelu, 1)
                    ring_split(s, R_U // 2 + i + 2)
                    act.wait_ge(u_prod, START + m + 1)
                    op_split(m, 0)
            act.wait_ge(vs_ready, 1)
            act.dma_start(v_sample[0, :, 0, :], v_smp[0:NS, 0:D]).then_inc(vs_out, 16)

            act.activation(warm, eps, ACT.Sigmoid)
            with act.Fori(0, KT) as m:
                act.wait_ge(acc_full, FREE + R_A + 2 * m + 1)
                act.wait_ge(a_out, START + m)
                act.activation(chunks(act_out[:, 0:TOK]), group(0), ACT.Sigmoid).then_inc(a_sig, 1)
                ring_split(0, R_A // 2 + m + 2)
                act.wait_ge(acc_full, FREE + R_A + 2 * m + 2)
                ring_split(1, R_A // 2 + m + 2)

            act.wait_ge(a_out, START + KT)
            with act.Fori(0, KT // 2) as i:
                for n in range(2):
                    m = 2 * i + n
                    act.wait_ge(acc_full, FREE + R_C + 6 * i + 3 * n + 1)
                    act.wait_ge(cx_done, START + m)
                    act.activation(chunks(act_out[:, 0:TOK]), group(n), ACT.Copy).then_inc(c_copied, 1)
                    for u in range(3):
                        at = 3 * n + u
                        if u:
                            act.wait_ge(acc_full, FREE + R_C + 6 * i + at + 1)
                        ring_split(at % 2, R_C // 2 + 3 * i + at // 2 + 2)
                    act.wait_ge(c_prod, START + m + 1)
                    op_split(m, KT)

            act.wait_ge(tail_turned, 1)
            act.activation(tail_out[:, :], ps[0:(2 + NS) * KT, 6, 0:128], ACT.Copy).then_inc(tail_copied, 1)
            act.wait_ge(tail_copied, 1)
            act.dma_start(conv_prompt[0, 0].rearrange("t (k p) -> (t k) p", p=128), tail_out[0:2 * KT, :]).then_inc(tail_saved, 16)
            for b in range(NS):
                act.dma_start(conv_sample[0, b, 1, :].rearrange("(k p) -> k p", p=128),
                              tail_out[KT * (2 + b):KT * (3 + b), :]).then_inc(tail_saved, 16)
            act.activation(warm, eps, ACT.Sigmoid)

            def b_gate(m):
                act.wait_ge(acc_full, FREE + R_B + 2 * m + 1)
                act.wait_ge(b_out, START + m)
                act.activation(chunks(act_out[:, 0:TOK]), group(0), ACT.Sigmoid).then_inc(b_sig, 1)

            with act.Fori(0, KT - 1) as m:
                b_gate(m)
                ring_split(0, R_B // 2 + m + 2)
                act.wait_ge(acc_full, FREE + R_B + 2 * m + 2)
                ring_split(1, R_B // 2 + m + 2)
            b_gate(KT - 1)
            for m in range(KT):
                act.wait_ge(h_sum, START + m + 1)
                act.activation(xn_hi[:, m, :], g[:, m, :], ACT.Copy).then_inc(h_hi, 1)

            def sqrt(n, c):
                act.wait_ge(n_base, 2 * c + n + 1)
                act.activation(tmp[5][:, CW:2 * CW], tmp[5][:, 0:CW], ACT.Sqrt).then_inc(n_sqrt, 1)

            def o_norm(c, step):
                t = slice(CW * c, CW * c + CW)
                if step == 0:
                    sqrt(0, c)
                elif step == 1:
                    act.wait_ge(x1_done, KT * (c + 1))
                    act.activation(g[:, :, t], xt[:, :, t], ACT.Square).then_inc(x1_sq, 1)
                elif step == 2:
                    sqrt(1, c)
                else:
                    act.wait_ge(x1n_ready, KT * (c + 1))
                    act.activation(xn_hi[:, :, t], g[:, :, t], ACT.Copy).then_inc(x1n_hi, 1)

            act.activation(warm, eps, ACT.Sqrt)
            for c in range(CH):
                for m in range(KT):
                    n = KT * c + m
                    act.wait_ge(acc_full, FREE + R_O + n + 1)
                    act.activation(g[:, m, CW * c:CW * c + CW], ps[:, n % 6, 0:CW], ACT.Copy).then_inc(o_copied, 1)
                    act.wait_ge(o_copied, n + 1)
                    if n >= 2:
                        act.wait_ge(o_acc, n - 1)
                    act.activation(tmp[n % 2][:, 0:CW], g[:, m, CW * c:CW * c + CW], ACT.Square).then_inc(o_sq, 1)
                    if c and m in (0, 3, 5, 7):
                        o_norm(c - 1, (0, 3, 5, 7).index(m))
            for step in range(4):
                o_norm(CH - 1, step)

            act.activation(warm, eps, ACT.Silu)

            def gate(j, i):
                act.activation(chunks(act_out[:, 0:TOK]), group(0), ACT.Silu).then_inc(f_silu, 1)

            def hidden(j, i):
                act.wait_ge(f_prod, 2 * j + i + 1)
                act.activation(flat2(hid, (j % 2) * 2 + i), prod[:, 0:TOK], ACT.Copy).then_inc(hid_hi, 1)

            for i in range(2):
                act.wait_ge(acc_full, FREE + R_F + 2 * i + 1)
                if i:
                    act.wait_ge(f_prod, 1)
                gate(0, i)
                ring_split(0, R_F // 2 + i + 2)
                act.wait_ge(acc_full, FREE + R_F + 2 * i + 2)
                ring_split(1, R_F // 2 + i + 2)
                hidden(0, i)
            with act.Fori(1, PAIRS) as j:
                for i in range(2):
                    act.wait_ge(acc_full, FREE + R_LOOP - 12 + 12 * j + 2 * i + 1)
                    act.wait_ge(f_prod, 2 * j + i)
                    gate(j, i)
                    ring_split(0, R_LOOP // 2 - 3 + 3 * j + i + 2)
                    act.wait_ge(acc_full, FREE + R_LOOP - 12 + 12 * j + 2 * i + 2)
                    ring_split(1, R_LOOP // 2 - 3 + 3 * j + i + 2)
                    hidden(j, i)
                for half in range(2):
                    act.wait_ge(acc_full, FREE + R_LOOP - 12 + 12 * j + 8 + 4 * half)
                    ring_split(half, R_LOOP // 2 - 3 + 3 * j + 4)

            for t in range(9):
                rows, _ = tokens(t)
                act.wait_ge(y_turned, t + 1)
                if t:
                    act.wait_ge(y_sumsq, t)
                act.activation(tmp[3][0:rows, 0:D].rearrange("p (a n) -> p a n", a=2),
                               ps[0:rows, 2 * (t % 2):2 * (t % 2) + 2, :], ACT.Square,
                               accum_out=small[0:rows, 9 + t:10 + t]).then_inc(y_sumsq, 1)

        @block.vector
        def _(dve):
            links = [0]

            def link(ins):
                links[0] += 1
                ins.then_inc(chain, 1)
                dve.wait_ge(chain, links[0])

            def rsqrt(y, a, t):
                link(dve.tensor_scalar(y.bitcast(i32), a.bitcast(i32), -0.5, float(0x5F3759DF), MUL, ADD))
                for _ in range(3):
                    link(dve.tensor_tensor(t, y, y, MUL))
                    link(dve.scalar_tensor_tensor(t, t, -0.5, a, MUL, MUL))
                    link(dve.scalar_tensor_tensor(y, t, 1.5, y, ADD, MUL))

            def scale_rows(t):
                rows, _ = tokens(t)
                a, y, w = (small[0:rows, 20 + n:21 + n] for n in range(3))
                dve.wait_ge(sumsq, t + 1)
                link(dve.tensor_scalar(a, small[0:rows, t:t + 1], 1.0 / D, EPS, MUL, ADD))
                rsqrt(y, a, w)
                dve.wait_ge(pre_in, 16)
                dve.scalar_tensor_tensor(x_norm[0:rows, 0:D], x_rows[t % 2][0:rows, 0:D], y,
                                         pre_gain[0:rows, 0:D], MUL, MUL).then_inc(x_scaled, 1)

            def wv_rest(k):
                dve.wait_ge(wv_hi, k + 1)
                dve.tensor_tensor(op_lo[:, k, 0:D], gv[:, k, :], op_hi[:, k, 0:D].bitcast(f32), SUB).then_inc(wv_lo, 1)

            def xn_rest(t):
                rows, at = tokens(t)
                dve.wait_ge(xn_hi_done, t + 1)
                dve.tensor_tensor(xn_lo[:, :, at:at + rows], bank_pair(6, rows),
                                  xn_hi[:, :, at:at + rows].bitcast(f32), SUB).then_inc(xn_lo_done, 1)

            def v_layer_norm(t):
                rows, _ = tokens(t)
                v = gv[:, t, :] if t < 8 else v_smp[0:NS, 0:D]
                dve.wait_ge(v_gelu, t + 1)
                dve.bn_stats(small[0:rows, 24:30], v[:, 0:512])
                link(dve.bn_stats(small[0:rows, 30:36], v[:, 512:1024]))
                link(dve.bn_aggr(small[0:rows, 36:38], small[0:rows, 24:36]))
                a, y, w = (small[0:rows, 40 + n:41 + n] for n in range(3))
                link(dve.tensor_scalar(a, small[0:rows, 37:38], EPS, None, ADD))
                rsqrt(y, a, w)
                dve.tensor_scalar(v, v, small[0:rows, 36:37], y, SUB, MUL).then_inc(v_norm, 1)

            for counted in (u_prod, op_lo_done, a_out, cx_done, c_prod, b_out, h_sum):
                dve.sem_inc(counted, START)
            scale_rows(0)
            for k in range(3):
                wv_rest(k)
            xn_rest(0)
            scale_rows(1)
            for k in range(3, KT):
                wv_rest(k)
            xn_rest(1)
            for t in range(9):
                if t + 2 < 9:
                    scale_rows(t + 2)
                v_layer_norm(t)
                if t + 2 < 9:
                    xn_rest(t + 2)
                if t == 7:
                    dve.wait_ge(const_turned, 1)
                    dve.tensor_copy(par[:, :], ps[:, 4, 0:P_ROWS])
                    dve.tensor_copy(hist[:, :, :, :].rearrange("p k t b -> p (k t b)"), ps[:, 4, 128:256]).then_inc(par_copied, 1)
            dve.wait_ge(v_norm, 9)
            dve.wait_ge(ln_g_in, 16)
            dve.wait_ge(ln_b_in, 16)
            link(dve.tensor_tensor(v_smp[0:NS, 0:D], v_smp[0:NS, 0:D], ln_g[0:NS, 0:D], MUL))
            dve.tensor_tensor(v_smp[0:NS, 0:D], v_smp[0:NS, 0:D], ln_b[0:NS, 0:D], ADD).then_inc(vs_ready, 1)

            def over_tokens(row, m):
                return row[:, ds(m * 128, 128)].unsqueeze(1).to_broadcast((128, 8, 128))

            def head(m):
                dst = v_head[:, 0:D].rearrange("p (n d) -> p n d", n=8)
                dve.wait_ge(mixed, START + m)
                dve.tensor_tensor(dst, gv[:, :, ds(m * 128, 128)], over_tokens(ln_g, m), MUL).then_inc(head_scaled, 1)
                dve.wait_ge(head_scaled, m + 1)
                dve.tensor_tensor(dst, dst, over_tokens(ln_b, m), ADD).then_inc(head_ready, 1)

            dve.wait_ge(vs_turned, 1)
            dve.wait_ge(ws00_in, 16)
            dve.wait_ge(b_in, 16)
            link(dve.tensor_tensor(mix_s[:, :, :], ps[:, 7, 0:NS * KT].rearrange("p (k b) -> p k b", k=KT),
                                   ws00[:, :].unsqueeze(2).to_broadcast((128, KT, NS)), MUL))
            dve.tensor_tensor(mix_s[:, :, :], mix_s[:, :, :],
                              b_rows[:, 0:D].rearrange("p (h i) -> p h i", h=KT)[:, :, 0:1].to_broadcast((128, KT, NS)), ADD) \
                .then_inc(mix_s_ready, 1)
            dve.wait_ge(mix_s_ready, 1)

            def op_rest(m, before):
                dve.wait_ge(op_hi_done, before + m + 1)
                dve.tensor_tensor(flat2(op_lo, m), prod[:, 0:TOK], flat2(op_hi, m).bitcast(f32), SUB).then_inc(op_lo_done, 1)

            with dve.Fori(0, KT) as m:
                head(m)
                smp, prm = slice(0, NS), slice(NS, TOK)
                dve.wait_ge(mixed, START + m + 1)
                dve.wait_ge(op_lo_done, START + m)
                dve.tensor_tensor(prod[:, prm].rearrange("p (n d) -> p n d", n=8), bank_pair(6), over_tokens(b_rows, m), ADD) \
                    .then_inc(mix_biased, 1)
                dve.wait_ge(u_gelu, m + 1)
                dve.wait_ge(mix_biased, m + 1)
                dve.tensor_tensor(prod[:, smp], act_out[:, smp], flat2(mix_s, m), MUL)
                dve.tensor_tensor(prod[:, prm], prod[:, prm], act_out[:, prm], MUL).then_inc(u_prod, 1)
                op_rest(m, 0)

            with dve.Fori(0, KT) as m:
                dve.wait_ge(acc_full, FREE + R_A + 2 * m + 2)
                dve.wait_ge(a_sig, START + m + 1)
                dve.tensor_tensor(flat3(g, m), group(1), chunks(act_out[:, 0:TOK]), MUL).then_inc(a_out, 1)

            link(dve.memset(c_in[:, 0:2], 0.0))
            with dve.Fori(0, KT // 2) as i:
                for n in range(2):
                    m = 2 * i + n
                    x_grp, b_grp = (3 * n + 1) % 2, (3 * n + 2) % 2
                    xg, p0 = group(x_grp), slice(NS, CW)
                    dve.wait_ge(acc_full, FREE + R_C + 6 * i + 3 * n + 2)
                    dve.wait_ge(c_copied, m + 1)
                    dve.tensor_tensor(tail[:, 2:2 + NS, ds(m, 1)].rearrange("p j a -> p (j a)"), xg[:, 0, 0:NS], act_out[:, 0:NS], MUL)
                    dve.tensor_tensor(c_in[:, 2:2 + CW - NS], xg[:, 0, p0], act_out[:, p0], MUL)
                    dve.tensor_tensor(c_in[:, 2 + CW - NS:2 + SEQ].rearrange("p (c w) -> p c w", c=2), xg[:, 1:3, :],
                                      act_out[:, CW:TOK].rearrange("p (c w) -> p c w", c=2), MUL).then_inc(cx_done, 1)
                    dve.wait_ge(cx_done, START + m + 1)
                    dve.wait_ge(op_hi_done, KT + m)
                    dve.tensor_copy(tail[:, 0:2, ds(m, 1)].rearrange("p j a -> p (j a)"), c_in[:, SEQ:SEQ + 2])
                    smp = (hist[:, ds(m, 1), 0, :], hist[:, ds(m, 1), 1, :], tail[:, 2:2 + NS, ds(m, 1)].rearrange("p j a -> p a j"))
                    out_s = prod[:, 0:NS].unsqueeze(1)
                    for k in range(3):
                        tap = par[:, ds(P_CONV + KT * k + m, 1)]
                        if k:
                            dve.wait_ge(conv_step, 2 * m + k)
                            dve.scalar_tensor_tensor(out_s, smp[k], tap, out_s, MUL, ADD)
                            ins = dve.scalar_tensor_tensor(prod[:, NS:TOK], c_in[:, k:k + SEQ], tap, prod[:, NS:TOK], MUL, ADD)
                        else:
                            dve.tensor_scalar(out_s, smp[k], tap, None, MUL)
                            ins = dve.tensor_scalar(prod[:, NS:TOK], c_in[:, k:k + SEQ], tap, None, MUL)
                        if k < 2:
                            ins.then_inc(conv_step, 1)
                    ins.then_inc(h_conv, 1)
                    dve.wait_ge(h_conv, m + 1)
                    dve.wait_ge(acc_full, FREE + R_C + 6 * i + 3 * n + 3)
                    dve.tensor_tensor(chunks(prod[:, 0:TOK]), group(b_grp), chunks(prod[:, 0:TOK]), MUL).then_inc(c_prod, 1)
                    op_rest(m, KT)

            def b_combine(m):
                dve.wait_ge(acc_full, FREE + R_B + 2 * m + 2)
                dve.wait_ge(b_sig, START + m + 1)
                dve.wait_ge(h_sum, START + m)
                dve.tensor_tensor(chunks(prod[:, 0:TOK]), group(1), chunks(act_out[:, 0:TOK]), MUL).then_inc(b_out, 1)
                dve.wait_ge(b_out, START + m + 1)
                dve.tensor_tensor(flat2(g, m), flat2(g, m), prod[:, 0:TOK], ADD).then_inc(h_sum, 1)

            def h_rest(m):
                dve.wait_ge(h_hi, m + 1)
                dve.tensor_tensor(xn_lo[:, m, :], g[:, m, :], xn_hi[:, m, :].bitcast(f32), SUB).then_inc(h_lo, 1)

            dve.wait_ge(op_lo_done, START + 2 * KT)
            with dve.Fori(0, KT - 1) as m:
                b_combine(m)
            for m in range(KT - 1):
                h_rest(m)
            b_combine(KT - 1)
            h_rest(KT - 1)

            base_t, root, inv, work = (tmp[5][:, 0:CW], tmp[5][:, CW:2 * CW], tmp[5][:, 2 * CW:3 * CW], tmp[6][:, 0:CW])

            def o_rsqrt(n, c):
                dve.wait_ge(n_sum, 2 * c + n + 1)
                dve.tensor_scalar(base_t, ps[:, 6 + n, 0:CW], 1.0 / D, EPS, MUL, ADD).then_inc(n_base, 1)
                dve.wait_ge(n_sqrt, 2 * c + n + 1)
                link(dve.reciprocal(inv, root))
                link(dve.tensor_tensor(work, inv, inv, MUL))
                link(dve.scalar_tensor_tensor(work, work, -0.5, base_t, MUL, MUL))
                link(dve.scalar_tensor_tensor(inv, work, 1.5, inv, ADD, MUL))

            def o_norm(c):
                t = slice(CW * c, CW * c + CW)
                gc, xc = g[:, :, t], xt[:, :, t]
                o_rsqrt(0, c)
                link(dve.tensor_tensor(gc, gc, inv.unsqueeze(1).to_broadcast((128, KT, CW)), MUL))
                yield
                dve.wait_ge(xt_in, 16)
                for m in range(KT):
                    dve.scalar_tensor_tensor(xt[:, m, t], g[:, m, t], par[:, P_POST + m:P_POST + m + 1], xt[:, m, t], MUL, ADD) \
                        .then_inc(x1_done, 1)
                    if m == 3:
                        yield
                yield
                dve.wait_ge(x1_sq, c + 1)
                dve.tensor_reduce(tmp[4][:, 0:CW], gc.rearrange("p m n -> p n m"), mybir.AxisListType.X, ADD).then_inc(x1_total, 1)
                yield
                yield
                o_rsqrt(1, c)
                yield
                for m in range(KT):
                    dve.scalar_tensor_tensor(g[:, m, t], xt[:, m, t], par[:, P_PRE + m:P_PRE + m + 1], inv, MUL, MUL) \
                        .then_inc(x1n_ready, 1)
                    if m == 3:
                        yield
                yield
                dve.wait_ge(x1n_hi, c + 1)
                dve.tensor_tensor(xn_lo[:, :, t], gc, xn_hi[:, :, t].bitcast(f32), SUB).then_inc(x1n_lo, 1)
                yield

            dve.wait_ge(vs_out, 16)
            steps = iter(())
            for c in range(CH):
                for m in range(KT):
                    n = KT * c + m
                    dve.wait_ge(o_sq, n + 1)
                    if m == 0:
                        if c:
                            dve.wait_ge(n_sum, 2 * c - 1)
                        dve.tensor_copy(tmp[3][:, 0:CW], tmp[n % 2][:, 0:CW]).then_inc(o_acc, 1)
                    else:
                        dve.wait_ge(o_acc, n)
                        dve.tensor_tensor(tmp[3][:, 0:CW], tmp[3][:, 0:CW], tmp[n % 2][:, 0:CW], ADD).then_inc(o_acc, 1)
                    next(steps, None)
                for _ in steps:
                    pass
                steps = o_norm(c)
            for _ in steps:
                pass

            dve.wait_ge(x1n_lo, CH)
            dve.memset(g[:, :, :], 0.0).then_inc(f_acc, START + 1)

            def hidden(j, i):
                dve.wait_ge(hid_lo, 2 * j + i)
                dve.tensor_tensor(chunks(prod[:, 0:TOK]), group(1), chunks(act_out[:, 0:TOK]), MUL).then_inc(f_prod, 1)
                dve.wait_ge(f_prod, 2 * j + i + 1)
                dve.wait_ge(hid_hi, 2 * j + i + 1)
                at = (j % 2) * 2 + i
                dve.tensor_tensor(flat2(hid, at + 4), prod[:, 0:TOK], flat2(hid, at).bitcast(f32), SUB).then_inc(hid_lo, 1)

            def add_down(j, before):
                for m in range(KT):
                    dve.wait_ge(acc_full, before + m + 1)
                    dve.wait_ge(f_acc, START + 8 * j - 7)
                    dst = g[:, m, :].rearrange("p (c w) -> p c w", c=CH)
                    dve.tensor_tensor(dst, dst, group(m % 2), ADD).then_inc(f_acc, 1)

            for i in range(2):
                dve.wait_ge(acc_full, FREE + R_F + 2 * i + 2)
                dve.wait_ge(f_silu, i + 1)
                hidden(0, i)
            with dve.Fori(1, PAIRS) as j:
                for i in range(2):
                    dve.wait_ge(acc_full, FREE + R_LOOP - 12 + 12 * j + 2 * i + 2)
                    dve.wait_ge(f_silu, 2 * j + i + 1)
                    hidden(j, i)
                add_down(j, FREE + R_LOOP - 12 + 12 * j + 4)
            add_down(PAIRS, base(PAIRS))

            dve.wait_ge(post_in, 16)
            for t in range(9):
                rows, _ = tokens(t)
                a, y, w = (small[0:rows, 44 + n:45 + n] for n in range(3))
                dst = tmp[5 + t % 2][0:rows, 0:D].rearrange("p (a n) -> p a n", a=2)
                dve.wait_ge(y_sumsq, t + 1)
                link(dve.tensor_scalar(a, small[0:rows, 9 + t:10 + t], 1.0 / D, EPS, MUL, ADD))
                rsqrt(y, a, w)
                if t >= 2:
                    dve.wait_ge(y_out[t % 2], 16 * (t // 2))
                dve.scalar_tensor_tensor(dst, ps[0:rows, 2 * (t % 2):2 * (t % 2) + 2, :], y,
                                         tmp[7][0:rows, 0:D].rearrange("p (a n) -> p a n", a=2), MUL, MUL).then_inc(y_scaled, 1)
                dve.wait_ge(y_scaled, t + 1)
                dve.tensor_tensor(dst, dst, ps[0:rows, 4 + 2 * (t % 2):6 + 2 * (t % 2), :], ADD).then_inc(y_ready, 1)


_INS = ["x_prompt", "x_sample", "state_conv", "mix_pre_g", "mix_post_g", "w_in", "sgu_ln_g", "sgu_ln_b", "w_s", "b_s",
        "conv_w", "w_a_out", "w_b_out", "w_o", "ffn_pre_g", "ffn_post_g", "w_gate", "w_up", "w_down"]
_OUTS = [("y_prompt", (1, SEQ, D)), ("y_sample", (NS, 1, D)), ("conv_prompt", (1, 1, 2, D)),
         ("conv_sample", (1, NS, 2, D)), ("v_sample", (1, NS, 1, D))]


def kernel(**inputs):
    import concourse.bacc as bacc
    from concourse.bass_utils import run_bass_kernel_spmd as run

    nc = bacc.Bacc("TRN2", target_bir_lowering=False, num_devices=1, dynamic_dma_scratch_size=1024)
    arrays, args = {}, {}
    for name in _INS:
        a = np.ascontiguousarray(inputs[name])
        arrays["in_" + name] = a
        args[name] = nc.dram_tensor("in_" + name, a.shape, mybir.dt.from_np(a.dtype), kind="ExternalInput").ap()
    for name, shape in _OUTS:
        args[name] = nc.dram_tensor("out_" + name, shape, mybir.dt.float32, kind="ExternalOutput").ap()
    build(nc, **args)
    r = run(nc, [arrays], core_ids=[0])
    return tuple(r.results[0]["out_" + name] for name, _ in _OUTS)
```

```python
from contextlib import ExitStack

import numpy as np

import concourse.bass as bass
from concourse import mybir

D = 1024
SEQ = 1024
NS = 8
TOK = NS + SEQ
KT = D // 128
CH = 3
CW = TOK // CH
FFN = 2816
EPS = 1e-6
PAIRS = FFN // 256
COL_U, COL_V, COL_B, COL_C, COL_X, COL_RA, COL_RB = (i * D for i in range(7))

R_U = 0
R_A = R_U + KT
R_C = R_A + 2 * KT
R_B = R_C + 3 * KT
R_O = R_B + 2 * KT
R_F = R_O + CH * KT
R_LOOP = R_F + 4
R_END = R_F + 6 * PAIRS
FREE = 9

START = 1

P_POST, P_PRE, P_OUT, P_CONV, P_ROWS = 0, KT, 2 * KT, 3 * KT, 6 * KT

O_SLOTS, O_STAGES, O_UNITS = 6, 4, CH * KT
Y_TILES = [8, 0, 1, 2, 3, 4, 5, 6, 7]


def build(nc, x_prompt, x_sample, state_conv, mix_pre_g, mix_post_g, w_in, sgu_ln_g, sgu_ln_b, w_s,
          b_s, conv_w, w_a_out, w_b_out, w_o, ffn_pre_g, ffn_post_g, w_gate, w_up, w_down,
          y_prompt, y_sample, conv_prompt, conv_sample, v_sample):
    f32, f32r, i32 = mybir.dt.float32, mybir.dt.float32r, mybir.dt.int32
    ALU, ACT = mybir.AluOpType, mybir.ActivationFunctionType
    MUL, ADD, SUB = ALU.mult, ALU.add, ALU.subtract
    ds = bass.ds

    xt_dram = nc.dram_tensor("xt_dram", [128, KT, TOK], f32, kind="Internal").ap()

    ctx = ExitStack()
    with ctx:
        def sb(name, shape, dt=f32):
            return ctx.enter_context(nc.sbuf_tensor(name, shape, dt))

        def sem(name):
            return ctx.enter_context(nc.semaphore(name))

        tile_bytes = KT * TOK * 4
        op_at = (nc.sbuf_usable_end - 2 * tile_bytes) // 32 * 32
        xn_at = op_at - 2 * tile_bytes
        xn_hi = nc.alloc_sbuf_tensor_at("xn_hi", [128, KT, TOK], f32r, offset=xn_at)
        xn_lo = nc.alloc_sbuf_tensor_at("xn_lo", [128, KT, TOK], f32r, offset=xn_at + tile_bytes)
        y_sq = nc.alloc_sbuf_tensor_at("y_sq", [128, KT, TOK], f32, offset=xn_at)
        x1_rows = nc.alloc_sbuf_tensor_at("x1_rows", [128, 8, D], f32, offset=xn_at + tile_bytes)
        op_hi = nc.alloc_sbuf_tensor_at("op_hi", [128, KT, TOK], f32r, offset=op_at)
        op_lo = nc.alloc_sbuf_tensor_at("op_lo", [128, KT, TOK], f32r, offset=op_at + tile_bytes)
        xt = nc.alloc_sbuf_tensor_at("xt", [128, KT, TOK], f32, offset=op_at)
        hid = op_lo
        g = sb("g", [128, KT, TOK])
        gv = g[:, :, 0:D]
        stage = [sb(f"stage{i}", [128, D]) for i in range(2)]
        ring_hi = [sb(f"ring_hi{i}", [128, D], f32r) for i in range(2)]
        ring_lo = [sb(f"ring_lo{i}", [128, D], f32r) for i in range(2)]
        tmp = [sb(f"tmp{i}", [128, TOK + 2]) for i in range(8)]
        ident = sb("ident", [128, 128])
        ones = sb("ones", [128, 128])
        par_rows = sb("par_rows", [P_ROWS, 128])
        par = sb("par", [128, P_ROWS])
        hist = sb("hist", [128, KT, 2, NS])
        ws00 = sb("ws00", [128, KT])
        mix_s = sb("mix_s", [128, KT, NS])
        tail = sb("tail", [128, 2 + NS, KT])
        tail_out = sb("tail_out", [(2 + NS) * KT, 128])
        small = sb("small", [128, 64])
        assert nc.sbuf_base <= xn_at, (nc.sbuf_base, xn_at)
        eps = small[:, 60:61]
        warm = small[:, 61:62]
        ps = ctx.enter_context(nc.psum_tensor("ps", [128, 8, 512], f32))

        x_rows = [tmp[0], tmp[1]]
        x_norm, x_save, pre_gain, v_smp, ws_t, ws_rows = tmp[2:8]
        hist_rows = tmp[5]
        act_out, v_head, prod, ln_g, ln_b = tmp[0:5]
        b_rows = tmp[7]
        c_in = tmp[1]
        o_stage = [stage[0], stage[1], tmp[7], tmp[1]]
        o_ring = [(ring_hi[n][:, :], ring_lo[n][:, :]) for n in range(2)] \
            + [(op_lo[:, k, 0:D], op_lo[:, k + 1, 0:D]) for k in (2, 6, 0, 4)]
        o_sum, o_square = tmp[3][:, 0:CW], [tmp[3][:, CW:2 * CW], tmp[3][:, 2 * CW:3 * CW]]
        x1_sum = tmp[4][:, 0:CW]
        gain_diag = tmp[3][:, 0:D].rearrange("p (m n) -> p m n", m=KT)
        y_rows = [tmp[5], tmp[6], tmp[7]]

        def group(i):
            return ps[:, 3 * i:3 * i + 3, 0:CW]

        def chunks(ap):
            return ap.rearrange("p (c w) -> p c w", c=CH)

        def flat2(t, m):
            return t[:, ds(m, 1), :].rearrange("p a n -> p (a n)")

        def flat3(t, m):
            return t[:, ds(m, 1), :].rearrange("p a (c w) -> p (a c) w", c=CH)

        def bank_pair(b, n=128):
            return ps[:, b:b + 2, :].rearrange("p a (k c) -> p (a k) c", c=128)[:, :, 0:n]

        def tokens(t):
            return (128, NS + 128 * t) if t < 8 else (NS, 0)

        consts = sem("consts")
        x_in = [sem("x_in0"), sem("x_in1")]
        wv_in = [sem(f"wv_in{k}") for k in range(KT)]
        wv_hi, wv_lo = sem("wv_hi"), sem("wv_lo")
        pre_in, ws_in, row_in, ws00_in = sem("pre_in"), sem("ws_in"), sem("row_in"), sem("ws00_in")
        ws_masked = sem("ws_masked")
        sumsq, x_scaled = sem("sumsq"), sem("x_scaled")
        raw_turned, norm_turned = sem("raw_turned"), sem("norm_turned")
        raw_copied, xt_saved = sem("raw_copied"), sem("xt_saved")
        xn_hi_done, xn_lo_done = sem("xn_hi_done"), sem("xn_lo_done")
        v_gelu, v_norm = sem("v_gelu"), sem("v_norm")
        chain = sem("chain")
        const_turned, ws_copied, par_copied = sem("const_turned"), sem("ws_copied"), sem("par_copied")
        ln_g_in, ln_b_in, b_in = sem("ln_g_in"), sem("ln_b_in"), sem("b_in")
        vs_ready, vs_turned, vs_out, mix_s_ready = sem("vs_ready"), sem("vs_turned"), sem("vs_out"), sem("mix_s_ready")
        w_in_done = [sem("w_loaded0"), sem("w_loaded1")]
        w_hi, pool_hi, w_lo = sem("w_hi"), sem("pool_hi"), sem("w_lo")
        acc_full = sem("acc_full")
        u_gelu, head_scaled, head_ready = sem("u_gelu"), sem("head_scaled"), sem("head_ready")
        mixed, mix_biased, u_prod = sem("mixed"), sem("mix_biased"), sem("u_prod")
        op_hi_done, op_lo_done = sem("op_hi_done"), sem("op_lo_done")
        a_sig, a_out = sem("a_sig"), sem("a_out")
        c_copied, cx_done, conv_step, h_conv, c_prod = sem("c_copied"), sem("cx_done"), sem("conv_step"), sem("h_conv"), sem("c_prod")
        tail_turned, tail_copied, tail_saved, hist_saved = sem("tail_turned"), sem("tail_copied"), sem("tail_saved"), sem("hist_saved")
        b_sig, b_out, h_sum = sem("b_sig"), sem("b_out"), sem("h_sum")
        h_hi, h_lo = sem("h_hi"), sem("h_lo")
        xt_in = sem("xt_in")
        o_copied, o_sq, o_acc = sem("o_copied"), sem("o_sq"), sem("o_acc")
        n_sum, n_sqrt, n_base, n_step = sem("n_sum"), sem("n_sqrt"), sem("n_base"), sem("n_step")
        x1_done, x1_sq, x1_total, x1n_ready, x1n_hi, x1n_lo = sem("x1_done"), sem("x1_sq"), sem("x1_total"), sem("x1n_ready"), sem("x1n_hi"), sem("x1n_lo")
        f_silu, f_prod, hid_hi, hid_lo, f_acc = sem("f_silu"), sem("f_prod"), sem("hid_hi"), sem("hid_lo"), sem("f_acc")
        o_in = [sem(f"o_in{n}") for n in range(O_STAGES)]
        p0_silu, p0_prod, p0_hi, p0_lo = sem("p0_silu"), sem("p0_prod"), sem("p0_hi"), sem("p0_lo")
        diag_ready = sem("diag_ready")
        x1_turned, x1_rows_done = sem("x1_turned"), sem("x1_rows_done")
        y_acc, y_squared, y_mean = sem("y_acc"), sem("y_squared"), sem("y_mean")
        y_summed, y_turned, y_ready = sem("y_summed"), sem("y_turned"), sem("y_ready")
        y_out = [sem(f"y_out{n}") for n in range(3)]

        def pair(j):
            return 12 * j + FREE + R_F

        def token_source(y):
            t = Y_TILES[y]
            return x1_rows[:, t, :] if t < 8 else tmp[1][:, 0:D]

        def y_banks(y):
            return 6 if y in (6, 8) else 4

        block = ctx.enter_context(nc.Block())

        @block.sync
        def _(sp):
            def x_load(t):
                rows, _ = tokens(t)
                if t >= 2:
                    sp.wait_ge(raw_turned, t - 1)
                    sp.wait_ge(x_scaled, t - 1)
                src = x_prompt[0, 128 * t:128 * t + 128, :] if t < 8 else x_sample[:, 0, :]
                sp.dma_start(x_rows[t % 2][0:rows, 0:D], src).then_inc(x_in[t % 2], 16)

            def wv_load(k):
                sp.dma_start(gv[:, k, :], w_in[0, 128 * k:128 * k + 128, COL_V:COL_V + D]).then_inc(wv_in[k], 16)

            def load(slot, src):
                sp.dma_start(stage[slot][:, :].rearrange("p (k c) -> p k c", k=src.shape[1]), src) \
                    .then_inc(w_in_done[slot], 16)

            def columns(w, at):
                return w.rearrange("(k p) n -> p k n", p=128)[:, :, ds(at, 128)]

            def down(j, half):
                return w_down[0].rearrange("(j k p) n -> p j k n", p=128, k=2)[:, ds(j, 1), :, 512 * half:512 * half + 512] \
                    .rearrange("p a k n -> p (a k) n")

            x_load(0)
            sp.dma_start(pre_gain[:, 0:D], mix_pre_g[0:1, :].to_broadcast((128, D))).then_inc(pre_in, 16)
            wv_load(0)
            wv_load(1)
            wv_load(2)
            x_load(1)
            for k in range(3, KT):
                wv_load(k)
            load(0, columns(w_in[0], COL_U))
            load(1, columns(w_in[0], COL_U + 128))
            for t in range(2, 9):
                x_load(t)
            sp.wait_ge(x_scaled, 9)
            sp.dma_start(ln_b[:, 0:D], sgu_ln_b[0:1, :].to_broadcast((128, D))).then_inc(ln_b_in, 16)
            sp.wait_ge(xt_saved, 16 * 9)
            sp.dma_start(ln_g[:, 0:D], sgu_ln_g[0:1, :].to_broadcast((128, D))).then_inc(ln_g_in, 16)
            sp.wait_ge(const_turned, 1)
            sp.dma_start(b_rows[:, 0:D], b_s[0:1].rearrange("a h i -> a (h i)").to_broadcast((128, D))).then_inc(b_in, 16)

            for m in range(2, KT):
                sp.wait_ge(w_lo, R_U + m - 1)
                load(m % 2, columns(w_in[0], COL_U + m * 128))
            with sp.Fori(1, KT + 1) as n:
                for s, (w, c0) in enumerate(((w_in[0], COL_RA), (w_a_out[0], 0))):
                    sp.wait_ge(w_lo, R_A + 2 * n - 2 + s - 1)
                    load(s, columns(w, n * 128 + c0 - 128))
            with sp.Fori(0, KT // 2) as i:
                for n in range(6):
                    at = sp.snap((COL_C, COL_X, COL_B)[n % 3] + n // 3 * 128 + i * 256)
                    sp.wait_ge(w_lo, R_C + 6 * i + n - 1)
                    load(n % 2, columns(w_in[0], at))
            with sp.Fori(1, KT + 1) as n:
                for s, (w, c0) in enumerate(((w_in[0], COL_RB), (w_b_out[0], 0))):
                    sp.wait_ge(w_lo, R_B + 2 * n - 2 + s - 1)
                    load(s, columns(w, n * 128 + c0 - 128))
            sp.wait_ge(op_lo_done, START + 2 * KT)
            for n in range(O_UNITS + 4):
                sp.wait_ge(w_lo, R_O + n + 1 - (O_STAGES if n >= O_STAGES else 2))
                src = columns(w_o[0], n % KT * 128) if n < O_UNITS else columns((w_gate, w_up)[n % 2][0], (n - O_UNITS) // 2 * 128)
                sp.dma_start(o_stage[n % O_STAGES][:, 0:D].rearrange("p (k c) -> p k c", k=KT), src).then_inc(o_in[n % O_STAGES], 16)
                if n == O_STAGES - 1:
                    sp.wait_ge(acc_full, FREE + R_O)
                    sp.dma_start(xt[:, :, :], xt_dram).then_inc(xt_in, 16)
            for n in range(4):
                sp.wait_ge(w_lo, R_LOOP + n - 1)
                load(n % 2, columns((w_gate, w_up)[n % 2][0], 256 + n // 2 * 128))
            with sp.Fori(1, PAIRS - 1) as j:
                for n in range(2):
                    before = sp.snap(j - 1)
                    sp.wait_ge(w_lo, R_LOOP + 6 * j - 2 + n - 1)
                    load(n, down(before, n))
                for n in range(4):
                    at = sp.snap(j * 256 + 256 + n // 2 * 128)
                    sp.wait_ge(w_lo, R_LOOP + 6 * j + n - 1)
                    load(n % 2, columns((w_gate, w_up)[n % 2][0], at))
            for n in range(4):
                sp.wait_ge(w_lo, R_LOOP + 6 * (PAIRS - 1) - 2 + n - 1)
                load(n % 2, down(PAIRS - 2 + n // 2, n % 2))

            for y, t in enumerate(Y_TILES):
                rows, _ = tokens(t)
                sp.wait_ge(y_ready, y + 1)
                dst = y_prompt[0, 128 * t:128 * t + 128, :] if t < 8 else y_sample[:, 0, :]
                sp.dma_start(dst, y_rows[y % 3][0:rows, 0:D]).then_inc(y_out[y % 3], 16)
            for n in range(3):
                sp.wait_ge(y_out[n], 16 * 3)
            sp.wait_ge(vs_out, 16)
            sp.wait_ge(hist_saved, 16)
            sp.wait_ge(tail_saved, 16 * (1 + NS))
            sp.wait_ge(xt_saved, 16 * 9)

        @block.gpsimd
        def _(pool):
            pool.memset(ident[:, :], 0.0).then_inc(consts, 1)
            pool.memset(ones[:, :], 1.0).then_inc(consts, 1)
            pool.memset(eps, EPS).then_inc(consts, 1)
            pool.wait_ge(consts, 3)
            pool.affine_select(out=ident[:, :], in_=ident[:, :], compare_op=ALU.not_equal, fill=1.0, base=0,
                               pattern=[[-1, 128]], channel_multiplier=1).then_inc(consts, 1)
            pool.wait_ge(ws_in, 16)
            wsv = ws_rows[:, 0:D].rearrange("p (h j) -> p h j", h=KT)
            pool.affine_select(out=wsv, in_=wsv, compare_op=ALU.is_ge, fill=0.0, base=0,
                               pattern=[[0, KT], [-1, 128]], channel_multiplier=1).then_inc(ws_masked, 1)

            def rest(src, hi, lo):
                pool.tensor_tensor(lo, src, hi.bitcast(f32), SUB).then_inc(w_lo, 1)

            for r in range(2):
                pool.wait_ge(w_in_done[r], 16)
                pool.tensor_copy(ring_hi[r][:, :], stage[r][:, :]).then_inc(pool_hi, 1)
                pool.wait_ge(pool_hi, r + 1)
                rest(stage[r][:, :], ring_hi[r][:, :], ring_lo[r][:, :])
            with pool.Fori(1, R_O // 2) as i:
                for s in range(2):
                    pool.wait_ge(w_hi, 2 * i + s - 1)
                    rest(stage[s][:, :], ring_hi[s][:, :], ring_lo[s][:, :])
            for n in range(O_UNITS + 4):
                pool.wait_ge(w_hi, R_O + n - 1)
                rest(o_stage[n % O_STAGES][:, 0:D], *o_ring[n % O_SLOTS])
            with pool.Fori(R_LOOP // 2, R_END // 2) as i:
                for s in range(2):
                    pool.wait_ge(w_hi, 2 * i + s - 1)
                    rest(stage[s][:, :], ring_hi[s][:, :], ring_lo[s][:, :])

        @block.tensor
        def _(pe):
            def three(out, w_h, w_l, x_h, x_l, first, last):
                ins = None
                for n, (w, x) in enumerate(((w_h, x_h), (w_h, x_l), (w_l, x_h))):
                    for o, xc in zip(out, x):
                        ins = pe.matmul(o, w, xc, start=first and n == 0, stop=last and n == 2)
                return ins

            def parts(x, k, n=CH):
                return [x[:, k, CW * c:CW * c + CW] for c in range(n)]

            def unit(slot, grp, x_h, x_l):
                out = [ps[:, 3 * grp + c, 0:CW] for c in range(CH)]
                for k in range(KT):
                    w = slice(128 * k, 128 * k + 128)
                    ins = three(out, ring_hi[slot][:, w], ring_lo[slot][:, w], parts(x_h, k), parts(x_l, k), k == 0, k == KT - 1)
                ins.then_inc(acc_full, 1)

            def turn(t):
                rows, _ = tokens(t)
                pe.wait_ge(x_in[t % 2], 16 * (t // 2 + 1))
                if t:
                    pe.wait_ge(raw_copied, t)
                for k in range(KT):
                    ins = pe.transpose(ps[:, 4 + k // 4, 128 * (k % 4):128 * (k % 4) + rows],
                                       x_rows[t % 2][0:rows, 128 * k:128 * k + 128], ident[0:rows, 0:rows])
                ins.then_inc(raw_turned, 1)
                pe.wait_ge(x_scaled, t + 1)
                if t:
                    pe.wait_ge(xn_lo_done, t)
                for k in range(KT):
                    ins = pe.transpose(ps[:, 6 + k // 4, 128 * (k % 4):128 * (k % 4) + rows],
                                       x_norm[0:rows, 128 * k:128 * k + 128], ident[0:rows, 0:rows])
                ins.then_inc(norm_turned, 1)

            def v_tile(t):
                _, at = tokens(t)
                pe.wait_ge(xn_lo_done, t + 1)
                if t >= 2:
                    pe.wait_ge(v_gelu, t - 1)
                out = [ps[:, 2 * (t % 2) + n, :] for n in range(2)]
                for k in range(KT):
                    if t == 0:
                        pe.wait_ge(wv_lo, k + 1)
                    w_h, w_l = ([w[:, k, 512 * n:512 * n + 512] for n in range(2)] for w in (op_hi, op_lo))
                    ins = three(out, xn_hi[:, k, at:at + 128], xn_lo[:, k, at:at + 128], w_h, w_l, k == 0, k == KT - 1)
                ins.then_inc(acc_full, 1)

            pe.sem_inc(mixed, START)
            pe.wait_ge(consts, 4)
            turn(0)
            turn(1)
            for t in range(9):
                v_tile(t)
                if t + 2 < 9:
                    turn(t + 2)
                if t == 7:
                    pe.wait_ge(raw_copied, 9)
                    pe.wait_ge(xn_lo_done, 9)
                    pe.wait_ge(row_in, 16 * 6)
                    pe.wait_ge(ws_masked, 1)
                    pe.transpose(ps[:, 4, 0:P_ROWS], par_rows[:, :], ident[0:P_ROWS, 0:P_ROWS])
                    for k in range(KT):
                        pe.transpose(ps[:, 4, 128 + 16 * k:144 + 16 * k], hist_rows[0:2 * NS, 128 * k:128 * k + 128],
                                     ident[0:2 * NS, 0:2 * NS])
                    for h in range(KT):
                        ins = pe.transpose(ps[:, 6 + h // 4, 128 * (h % 4):128 * (h % 4) + 128],
                                           ws_rows[:, 128 * h:128 * h + 128], ident[:, :])
                    ins.then_inc(const_turned, 1)
            pe.wait_ge(v_gelu, 8)
            pe.wait_ge(par_copied, 1)

            def mix(m):
                pe.wait_ge(head_ready, m + 1)
                pe.wait_ge(mix_biased, m)
                for n in range(8):
                    ins = pe.matmul(ps[:, 6 + n // 4, 128 * (n % 4):128 * (n % 4) + 128],
                                    v_head[:, 128 * n:128 * n + 128], ws_t[:, ds(m * 128, 128)], start=True, stop=True)
                ins.then_inc(mixed, 1)

            pe.wait_ge(w_lo, 1)
            unit(0, 1, xn_hi, xn_lo)
            pe.wait_ge(vs_ready, 1)
            pe.wait_ge(v_gelu, 9)
            for k in range(KT):
                ins = pe.transpose(ps[:, 0, NS * k:NS * k + NS], v_smp[0:NS, 128 * k:128 * k + 128], ident[0:NS, 0:NS])
            ins.then_inc(vs_turned, 1)
            pe.wait_ge(ws_copied, 1)
            mix(0)
            pe.wait_ge(w_lo, 2)
            pe.wait_ge(mix_s_ready, 1)
            unit(1, 0, xn_hi, xn_lo)
            mix(1)
            with nc.Fori(1, KT // 2, engines=[mybir.EngineType.PE], hint_back_edge=True) as i:
                for s in range(2):
                    m = 2 * i + s
                    pe.wait_ge(w_lo, R_U + m + 1)
                    pe.wait_ge(u_gelu, m - 1)
                    unit(s, 1 - s, xn_hi, xn_lo)
                    mix(m)

            pe.wait_ge(u_gelu, KT)
            with nc.Fori(0, KT, engines=[mybir.EngineType.PE], hint_back_edge=True) as m:
                pe.wait_ge(w_lo, R_A + 2 * m + 1)
                pe.wait_ge(a_sig, START + m)
                unit(0, 1, xn_hi, xn_lo)
                pe.wait_ge(w_lo, R_A + 2 * m + 2)
                pe.wait_ge(a_out, START + m)
                pe.wait_ge(op_lo_done, START + KT)
                unit(1, 0, op_hi, op_lo)

            with nc.Fori(0, KT // 2, engines=[mybir.EngineType.PE], hint_back_edge=True) as i:
                for n in range(6):
                    m = 2 * i + n // 3
                    pe.wait_ge(w_lo, R_C + 6 * i + n + 1)
                    if n % 3 == 0:
                        pe.wait_ge(cx_done, START + m)
                        if n == 0:
                            pe.wait_ge(a_sig, START + KT)
                    elif n % 3 == 1:
                        pe.wait_ge(c_prod, START + m)
                        if n == 1:
                            pe.wait_ge(a_out, START + KT)
                    else:
                        pe.wait_ge(c_copied, m + 1)
                    unit(n % 2, 1 - n % 2, xn_hi, xn_lo)

            pe.wait_ge(h_conv, KT)
            pe.transpose(ps[0:(2 + NS) * KT, 6, 0:128], tail[:, :, :].rearrange("p j m -> p (j m)"), ident[:, :]) \
                .then_inc(tail_turned, 1)
            with nc.Fori(0, KT, engines=[mybir.EngineType.PE], hint_back_edge=True) as m:
                pe.wait_ge(w_lo, R_B + 2 * m + 1)
                pe.wait_ge(b_sig, START + m)
                unit(0, 1, xn_hi, xn_lo)
                pe.wait_ge(w_lo, R_B + 2 * m + 2)
                pe.wait_ge(b_out, START + m)
                pe.wait_ge(op_lo_done, START + 2 * KT)
                unit(1, 0, op_hi, op_lo)

            def norm_sum(n, at):
                pe.matmul(ps[:, 6 + n % 2, 0:CW], ones[:, :], at, start=True, stop=True).then_inc(n_sum, 1)

            def first_norm(c):
                pe.wait_ge(o_acc, KT * (c + 1))
                norm_sum(0, tmp[3][:, 0:CW])

            def second_norm(c):
                pe.wait_ge(x1_total, c + 1)
                norm_sum(1, tmp[4][:, 0:CW])

            pe.wait_ge(b_out, START + KT)
            pe.wait_ge(tail_copied, 1)
            def chunk_unit(n, x_h, x_l, c, bank):
                w_h, w_l = o_ring[n % O_SLOTS]
                t = slice(CW * c, CW * c + CW)
                for k in range(KT):
                    w = slice(128 * k, 128 * k + 128)
                    ins = three([ps[:, bank, 0:CW]], w_h[:, w], w_l[:, w], [x_h[:, k, t]], [x_l[:, k, t]], k == 0, k == KT - 1)
                ins.then_inc(acc_full, 1)

            for c in range(CH):
                pe.wait_ge(h_lo, KT + c)
                for m in range(KT):
                    n = KT * c + m
                    pe.wait_ge(w_lo, R_O + n + 1)
                    if n in (1, 2):
                        pe.wait_ge(b_out, START + KT + n)
                    if n >= 6:
                        pe.wait_ge(o_copied, n - 5)
                    chunk_unit(n, xn_hi, xn_lo, c, n % 6)
                    if c and m == 0:
                        first_norm(c - 1)
                    if c and m == 5:
                        second_norm(c - 1)

            for c in range(CH):
                pe.wait_ge(x1n_lo, c + 1)
                for f in range(4):
                    n = 4 * c + f
                    pe.wait_ge(w_lo, R_F + f + 1)
                    if n < 6:
                        pe.wait_ge(o_copied, O_UNITS - 5 + n)
                    else:
                        pe.wait_ge((p0_silu, p0_prod)[n % 2], (n - 6) // 2 + 1)
                    chunk_unit(O_UNITS + f, xn_hi, xn_lo, c, n % 6)
                    if n == 0:
                        first_norm(CH - 1)
                    if n == 5:
                        second_norm(CH - 1)

            def down(j):
                pe.wait_ge(p0_lo, 6)
                pe.wait_ge(hid_lo, 2 * j)
                for m in range(KT):
                    slot = m // 4
                    if m % 4 == 0:
                        pe.wait_ge(w_lo, R_LOOP + 6 * (j - 1) + 4 + slot + 1)
                    if m < 2:
                        pe.wait_ge((f_silu, f_prod)[m], 2 * j + 2)
                    else:
                        pe.wait_ge(f_acc, START + 8 * j - 8 + m)
                    for k in range(2):
                        w = slice(512 * k + 128 * (m % 4), 512 * k + 128 * (m % 4) + 128)
                        at = ((j - 1) % 2) * 2 + k
                        x_h, x_l = ([hid[:, ds(o + at, 1), CW * c:CW * c + CW].rearrange("p a n -> p (a n)") for c in range(CH)]
                                    for o in (0, 4))
                        ins = three([ps[:, 3 * (m % 2) + c, 0:CW] for c in range(CH)],
                                    ring_hi[slot][:, w], ring_lo[slot][:, w], x_h, x_l, k == 0, k == 1)
                    ins.then_inc(acc_full, 1)

            with nc.Fori(1, PAIRS, engines=[mybir.EngineType.PE], hint_back_edge=True) as j:
                for n in range(4):
                    pe.wait_ge(w_lo, R_LOOP + 6 * (j - 1) + n + 1)
                    if n < 2:
                        pe.wait_ge(p0_silu, 5 + n)
                        if n:
                            pe.wait_ge(p0_prod, 6)
                        pe.wait_ge(f_acc, START + 8 * j - 8 + n)
                    pe.wait_ge((f_silu, f_prod)[n % 2], 2 * j + n // 2)
                    unit(n % 2, n % 2, xn_hi, xn_lo)
                down(j)

            def turn_x1(y):
                rows, at = tokens(Y_TILES[y])
                if y:
                    pe.wait_ge(x1_rows_done, y)
                for k in range(KT):
                    ins = pe.transpose(ps[0:rows, 6 + k // 4, 128 * (k % 4):128 * (k % 4) + 128], xt[:, k, at:at + rows], ident[:, :])
                ins.then_inc(x1_turned, 1)

            def turn_y(y):
                rows, at = tokens(Y_TILES[y])
                pe.wait_ge(y_squared, KT * (y // 3 + 1))
                if y:
                    pe.wait_ge(y_mean, y)
                for k in range(KT):
                    ins = pe.matmul(ps[0:rows, 3, y:y + 1], y_sq[:, k, at:at + rows], ones[:, 0:1], start=k == 0, stop=k == KT - 1)
                ins.then_inc(y_summed, 1)
                if y == 6:
                    pe.wait_ge(x1_rows_done, 9)
                elif y:
                    pe.wait_ge(y_ready, y if y < 6 else y - 1)
                b = y_banks(y)
                for k in range(KT):
                    ins = pe.matmul(ps[0:rows, b + k // 4, 128 * (k % 4):128 * (k % 4) + 128], g[:, k, at:at + rows],
                                    gain_diag[:, k, :], start=True, stop=True)
                ins.then_inc(y_turned, 1)

            pe.wait_ge(w_lo, R_END)
            pe.wait_ge(hid_lo, 2 * PAIRS)
            pe.wait_ge(f_acc, START + 1 + 8 * (PAIRS - 1))
            pe.wait_ge(diag_ready, 1)
            for q in range(CH * KT):
                c, m = divmod(q, KT)
                if q >= 3:
                    pe.wait_ge(y_acc, q - 2)
                for k in range(2):
                    w = slice(512 * k + 128 * (m % 4), 512 * k + 128 * (m % 4) + 128)
                    at = (PAIRS - 1) % 2 * 2 + k
                    t = slice(CW * c, CW * c + CW)
                    ins = three([ps[:, q % 3, 0:CW]], ring_hi[m // 4][:, w], ring_lo[m // 4][:, w],
                                [hid[:, at, t]], [hid[:, at + 4, t]], k == 0, k == 1)
                ins.then_inc(acc_full, 1)
                if q % 2 and q <= 17:
                    turn_x1(q // 2)
                if q >= 11 and q % 8 in (3, 5, 7):
                    turn_y((q - 8) // 8 * 3 + (q % 8 - 3) // 2)
            for y in range(6, 9):
                turn_y(y)

        @block.scalar
        def _(act):
            for counted in (a_sig, b_sig):
                act.sem_inc(counted, START)
            act.wait_ge(consts, 3)
            act.activation(warm, eps, ACT.Gelu_apprx_tanh)

            def square(t):
                rows, _ = tokens(t)
                act.wait_ge(x_in[t % 2], 16 * (t // 2 + 1))
                if t:
                    act.wait_ge(norm_turned, t)
                act.activation(x_norm[0:rows, 0:D], x_rows[t % 2][0:rows, 0:D], ACT.Square,
                               accum_out=small[0:rows, t:t + 1]).then_inc(sumsq, 1)

            def wv_split(k):
                act.wait_ge(wv_in[k], 16)
                act.activation(op_hi[:, k, 0:D], gv[:, k, :], ACT.Copy).then_inc(wv_hi, 1)

            def keep(t):
                rows, at = tokens(t)
                act.wait_ge(raw_turned, t + 1)
                if t:
                    act.wait_ge(xt_saved, 16 * t)
                saved = x_save[:, 0:KT * rows].rearrange("p (k n) -> p k n", k=KT)
                act.activation(saved, bank_pair(4, rows), ACT.Copy).then_inc(raw_copied, 1)
                act.wait_ge(norm_turned, t + 1)
                act.activation(xn_hi[:, :, at:at + rows], bank_pair(6, rows), ACT.Copy).then_inc(xn_hi_done, 1)
                act.wait_ge(raw_copied, t + 1)
                act.dma_start(xt_dram[:, :, at:at + rows], saved).then_inc(xt_saved, 16)

            square(0)
            wv_split(0)
            wv_split(1)
            keep(0)
            wv_split(2)
            square(1)
            for k in range(3, KT):
                wv_split(k)
            keep(1)
            for n, src in enumerate((mix_post_g, ffn_pre_g, ffn_post_g)):
                act.dma_start(par_rows[KT * n:KT * n + KT, :], src[0].rearrange("(k p) -> k p", p=128)).then_inc(row_in, 16)
            act.dma_start(par_rows[P_CONV:P_ROWS, :], conv_w[0].rearrange("w (k p) -> (w k) p", p=128)).then_inc(row_in, 16)
            for n in range(2):
                act.dma_start(hist_rows[NS * n:NS * n + NS, 0:D], state_conv[0, :, n, :]).then_inc(row_in, 16)
            act.dma_start(ws_rows[:, 0:D].rearrange("p (h j) -> p h j", h=KT), w_s[0].rearrange("h i j -> i h j")).then_inc(ws_in, 16)
            with nc.allow_non_contiguous_dma(reason="8 scalars to each partition"):
                act.dma_start(ws00[:, :], w_s[0, :, 0, 0:1].rearrange("h a -> a h").to_broadcast((128, KT))).then_inc(ws00_in, 16)
            act.dma_start(conv_sample[0, :, 0, :], state_conv[0, :, 1, :]).then_inc(hist_saved, 16)
            for t in range(9):
                if t + 2 < 9:
                    square(t + 2)
                act.wait_ge(acc_full, t + 1)
                rows, _ = tokens(t)
                if t < 8:
                    if t == 0:
                        act.wait_ge(wv_lo, KT)
                    dst = gv[:, t, :]
                else:
                    act.wait_ge(const_turned, 1)
                    dst = v_smp[0:NS, 0:D]
                act.activation(dst.rearrange("p (a n) -> p a n", a=2), ps[0:rows, 2 * (t % 2):2 * (t % 2) + 2, :],
                               ACT.Gelu_apprx_tanh).then_inc(v_gelu, 1)
                if t + 2 < 9:
                    keep(t + 2)
            act.wait_ge(const_turned, 1)
            act.activation(ws_t[:, 0:D].rearrange("p (k n) -> p k n", k=KT), bank_pair(6), ACT.Copy).then_inc(ws_copied, 1)

            def ring_split(s, loads):
                act.wait_ge(w_in_done[s], 16 * loads)
                act.activation(ring_hi[s][:, :], stage[s][:, :], ACT.Copy).then_inc(w_hi, 1)

            def op_split(m, n):
                act.activation(flat2(op_hi, m), prod[:, 0:TOK], ACT.Copy).then_inc(op_hi_done, 1)

            with act.Fori(0, KT // 2) as i:
                for s in range(2):
                    m = 2 * i + s
                    act.wait_ge(acc_full, FREE + R_U + m + 1)
                    act.wait_ge(u_prod, START + m)
                    act.activation(chunks(act_out[:, 0:TOK]), group(1 - s), ACT.Gelu_apprx_tanh).then_inc(u_gelu, 1)
                    ring_split(s, R_U // 2 + i + 2)
                    act.wait_ge(u_prod, START + m + 1)
                    op_split(m, 0)
            act.wait_ge(vs_ready, 1)
            act.dma_start(v_sample[0, :, 0, :], v_smp[0:NS, 0:D]).then_inc(vs_out, 16)

            act.activation(warm, eps, ACT.Sigmoid)
            with act.Fori(0, KT) as m:
                act.wait_ge(acc_full, FREE + R_A + 2 * m + 1)
                act.wait_ge(a_out, START + m)
                act.activation(chunks(act_out[:, 0:TOK]), group(1), ACT.Sigmoid).then_inc(a_sig, 1)
                ring_split(0, R_A // 2 + m + 2)
                act.wait_ge(acc_full, FREE + R_A + 2 * m + 2)
                ring_split(1, R_A // 2 + m + 2)

            act.wait_ge(a_out, START + KT)
            with act.Fori(0, KT // 2) as i:
                for n in range(2):
                    m = 2 * i + n
                    act.wait_ge(acc_full, FREE + R_C + 6 * i + 3 * n + 1)
                    act.wait_ge(cx_done, START + m)
                    act.activation(chunks(act_out[:, 0:TOK]), group(1 - n), ACT.Copy).then_inc(c_copied, 1)
                    for u in range(3):
                        at = 3 * n + u
                        if u:
                            act.wait_ge(acc_full, FREE + R_C + 6 * i + at + 1)
                        ring_split(at % 2, R_C // 2 + 3 * i + at // 2 + 2)
                    act.wait_ge(c_prod, START + m + 1)
                    op_split(m, KT)

            act.wait_ge(tail_turned, 1)
            act.activation(tail_out[:, :], ps[0:(2 + NS) * KT, 6, 0:128], ACT.Copy).then_inc(tail_copied, 1)
            act.wait_ge(tail_copied, 1)
            act.dma_start(conv_prompt[0, 0].rearrange("t (k p) -> (t k) p", p=128), tail_out[0:2 * KT, :]).then_inc(tail_saved, 16)
            for b in range(NS):
                act.dma_start(conv_sample[0, b, 1, :].rearrange("(k p) -> k p", p=128),
                              tail_out[KT * (2 + b):KT * (3 + b), :]).then_inc(tail_saved, 16)
            act.activation(warm, eps, ACT.Sigmoid)

            def b_gate(m):
                act.wait_ge(acc_full, FREE + R_B + 2 * m + 1)
                act.wait_ge(b_out, START + m)
                act.activation(chunks(act_out[:, 0:TOK]), group(1), ACT.Sigmoid).then_inc(b_sig, 1)

            with act.Fori(0, KT - 1) as m:
                b_gate(m)
                ring_split(0, R_B // 2 + m + 2)
                act.wait_ge(acc_full, FREE + R_B + 2 * m + 2)
                ring_split(1, R_B // 2 + m + 2)
            b_gate(KT - 1)
            def o_split(n):
                act.wait_ge(o_in[n % O_STAGES], 16 * (n // O_STAGES + 1))
                act.activation(o_ring[n % O_SLOTS][0], o_stage[n % O_STAGES][:, 0:D], ACT.Copy).then_inc(w_hi, 1)

            o_split(0)
            for m in range(KT - 1):
                act.wait_ge(h_sum, START + m + 1)
                act.activation(xn_hi[:, m, :], g[:, m, :], ACT.Copy).then_inc(h_hi, 1)
            for c in range(CH):
                t = slice(CW * c, CW * c + CW)
                act.wait_ge(h_sum, START + KT + c)
                act.activation(xn_hi[:, KT - 1, t], g[:, KT - 1, t], ACT.Copy).then_inc(h_hi, 1)
                o_split(c + 1)
            for n in range(CH + 1, O_SLOTS):
                o_split(n)

            def sqrt(n, c):
                act.wait_ge(n_base, 2 * c + n + 1)
                act.activation(tmp[5][:, CW:2 * CW], tmp[5][:, 0:CW], ACT.Sqrt).then_inc(n_sqrt, 1)

            def o_norm(c, step):
                t = slice(CW * c, CW * c + CW)
                if step in (0, 3):
                    sqrt(step // 3, c)
                    return
                n = 2 * c + (step - 1) % 3
                half = slice(KT // 2 * (n % 2), KT // 2 * (n % 2) + KT // 2)
                if step < 3:
                    act.wait_ge(x1_done, n + 1)
                    act.activation(g[:, half, t], xt[:, half, t], ACT.Square).then_inc(x1_sq, 1)
                else:
                    act.wait_ge(x1n_ready, n + 1)
                    act.activation(xn_hi[:, half, t], g[:, half, t], ACT.Copy).then_inc(x1n_hi, 1)

            act.activation(warm, eps, ACT.Sqrt)
            for c in range(CH):
                for m in range(KT):
                    n = KT * c + m
                    act.wait_ge(acc_full, FREE + R_O + n + 1)
                    act.activation(g[:, m, CW * c:CW * c + CW], ps[:, n % 6, 0:CW], ACT.Copy, scale=par[:, P_POST + m:P_POST + m + 1])
                    if n >= 2:
                        act.wait_ge(o_acc, n - 1)
                    act.activation(o_square[n % 2], ps[:, n % 6, 0:CW], ACT.Square).then_inc(o_copied, 1)
                    if n + O_SLOTS < O_UNITS + 4:
                        o_split(n + O_SLOTS)
                    if c:
                        for step in {0: (0,), 2: (1,), 3: (2,), 5: (3,), 6: (4,), 7: (5,)}.get(m, ()):
                            o_norm(c - 1, step)


            def gate(j, i):
                act.activation(chunks(act_out[:, 0:TOK]), group(0), ACT.Silu).then_inc(f_silu, 1)

            def hidden(j, i):
                act.wait_ge(f_prod, 2 * j + i + 1)
                act.activation(flat2(hid, (j % 2) * 2 + i), prod[:, 0:TOK], ACT.Copy).then_inc(hid_hi, 1)

            def first_gate(n):
                act.wait_ge(acc_full, FREE + R_F + 2 * n + 1)
                if n >= 3:
                    act.wait_ge(p0_prod, n - 2)
                act.activation(act_out[:, CW * (n % 3):CW * (n % 3) + CW], ps[:, 2 * n % 6, 0:CW], ACT.Silu).then_inc(p0_silu, 1)

            def first_hidden(n):
                t = slice(CW * (n // 2), CW * (n // 2) + CW)
                act.wait_ge(p0_prod, n + 1)
                act.activation(hid[:, n % 2, t], prod[:, CW * (n % 3):CW * (n % 3) + CW], ACT.Copy).then_inc(p0_hi, 1)

            o_norm(CH - 1, 0)
            first_gate(0)
            first_hidden(0)
            first_gate(1)
            first_hidden(1)
            for step in range(1, 6):
                o_norm(CH - 1, step)
            for n in range(2, 6):
                first_gate(n)
                if n >= 4:
                    act.wait_ge(acc_full, FREE + R_F + 9 + n - 4)
                    ring_split(n - 4, R_O // 2 + 1)
                first_hidden(n)
            for counted in (f_silu, hid_hi):
                act.sem_inc(counted, 2)
            with act.Fori(1, PAIRS) as j:
                for i in range(2):
                    act.wait_ge(acc_full, pair(j) + 2 * i + 1)
                    act.wait_ge(f_prod, 2 * j + i)
                    gate(j, i)
                    ring_split(0, R_O // 2 - 3 + 3 * j + i + 2)
                    act.wait_ge(acc_full, pair(j) + 2 * i + 2)
                    ring_split(1, R_O // 2 - 3 + 3 * j + i + 2)
                    hidden(j, i)
                for half in range(2):
                    act.wait_ge(acc_full, pair(j) + 8 + 4 * half)
                    ring_split(half, R_O // 2 - 3 + 3 * j + 4)

            for q in range(CH * KT):
                c, m = divmod(q, KT)
                t = slice(CW * c, CW * c + CW)
                act.wait_ge(y_acc, q + 1)
                act.activation(y_sq[:, m, t], g[:, m, t], ACT.Square).then_inc(y_squared, 1)
                if q % 2 and q <= 17:
                    x = q // 2
                    rows, _ = tokens(Y_TILES[x])
                    act.wait_ge(x1_turned, x + 1)
                    dst = token_source(x)
                    act.activation(dst[0:rows].rearrange("p (a n) -> p a n", a=2), ps[0:rows, 6:8, :], ACT.Copy).then_inc(x1_rows_done, 1)

        @block.vector
        def _(dve):
            links = [0]

            def link(ins):
                links[0] += 1
                ins.then_inc(chain, 1)
                dve.wait_ge(chain, links[0])

            def rsqrt(y, a, t):
                link(dve.tensor_scalar(y.bitcast(i32), a.bitcast(i32), -0.5, float(0x5F3759DF), MUL, ADD))
                for _ in range(3):
                    link(dve.tensor_tensor(t, y, y, MUL))
                    link(dve.scalar_tensor_tensor(t, t, -0.5, a, MUL, MUL))
                    link(dve.scalar_tensor_tensor(y, t, 1.5, y, ADD, MUL))

            def scale_rows(t):
                rows, _ = tokens(t)
                a, y, w = (small[0:rows, 20 + n:21 + n] for n in range(3))
                dve.wait_ge(sumsq, t + 1)
                link(dve.tensor_scalar(a, small[0:rows, t:t + 1], 1.0 / D, EPS, MUL, ADD))
                rsqrt(y, a, w)
                dve.wait_ge(pre_in, 16)
                dve.scalar_tensor_tensor(x_norm[0:rows, 0:D], x_rows[t % 2][0:rows, 0:D], y,
                                         pre_gain[0:rows, 0:D], MUL, MUL).then_inc(x_scaled, 1)

            def wv_rest(k):
                dve.wait_ge(wv_hi, k + 1)
                dve.tensor_tensor(op_lo[:, k, 0:D], gv[:, k, :], op_hi[:, k, 0:D].bitcast(f32), SUB).then_inc(wv_lo, 1)

            def xn_rest(t):
                rows, at = tokens(t)
                dve.wait_ge(xn_hi_done, t + 1)
                dve.tensor_tensor(xn_lo[:, :, at:at + rows], bank_pair(6, rows),
                                  xn_hi[:, :, at:at + rows].bitcast(f32), SUB).then_inc(xn_lo_done, 1)

            def v_layer_norm(t):
                rows, _ = tokens(t)
                v = gv[:, t, :] if t < 8 else v_smp[0:NS, 0:D]
                dve.wait_ge(v_gelu, t + 1)
                dve.bn_stats(small[0:rows, 24:30], v[:, 0:512])
                link(dve.bn_stats(small[0:rows, 30:36], v[:, 512:1024]))
                link(dve.bn_aggr(small[0:rows, 36:38], small[0:rows, 24:36]))
                a, y, w = (small[0:rows, 40 + n:41 + n] for n in range(3))
                link(dve.tensor_scalar(a, small[0:rows, 37:38], EPS, None, ADD))
                rsqrt(y, a, w)
                dve.tensor_scalar(v, v, small[0:rows, 36:37], y, SUB, MUL).then_inc(v_norm, 1)

            for counted in (u_prod, op_lo_done, a_out, cx_done, c_prod, b_out, h_sum):
                dve.sem_inc(counted, START)
            dve.sem_inc(f_acc, START + 1)
            scale_rows(0)
            for k in range(2):
                wv_rest(k)
            xn_rest(0)
            wv_rest(2)
            scale_rows(1)
            for k in range(3, KT):
                wv_rest(k)
            xn_rest(1)
            for t in range(9):
                if t + 2 < 9:
                    scale_rows(t + 2)
                v_layer_norm(t)
                if t + 2 < 9:
                    xn_rest(t + 2)
                if t == 7:
                    dve.wait_ge(const_turned, 1)
                    dve.tensor_copy(par[:, :], ps[:, 4, 0:P_ROWS])
                    dve.tensor_copy(hist[:, :, :, :].rearrange("p k t b -> p (k t b)"), ps[:, 4, 128:256]).then_inc(par_copied, 1)
            dve.wait_ge(v_norm, 9)
            dve.wait_ge(ln_g_in, 16)
            dve.wait_ge(ln_b_in, 16)
            link(dve.tensor_tensor(v_smp[0:NS, 0:D], v_smp[0:NS, 0:D], ln_g[0:NS, 0:D], MUL))
            dve.tensor_tensor(v_smp[0:NS, 0:D], v_smp[0:NS, 0:D], ln_b[0:NS, 0:D], ADD).then_inc(vs_ready, 1)

            def over_tokens(row, m):
                return row[:, ds(m * 128, 128)].unsqueeze(1).to_broadcast((128, 8, 128))

            def head(m):
                dst = v_head[:, 0:D].rearrange("p (n d) -> p n d", n=8)
                dve.wait_ge(mixed, START + m)
                dve.tensor_tensor(dst, gv[:, :, ds(m * 128, 128)], over_tokens(ln_g, m), MUL).then_inc(head_scaled, 1)
                dve.wait_ge(head_scaled, m + 1)
                dve.tensor_tensor(dst, dst, over_tokens(ln_b, m), ADD).then_inc(head_ready, 1)

            head(0)
            dve.wait_ge(vs_turned, 1)
            dve.wait_ge(ws00_in, 16)
            dve.wait_ge(b_in, 16)
            link(dve.tensor_tensor(mix_s[:, :, :], ps[:, 0, 0:NS * KT].rearrange("p (k b) -> p k b", k=KT),
                                   ws00[:, :].unsqueeze(2).to_broadcast((128, KT, NS)), MUL))
            dve.tensor_tensor(mix_s[:, :, :], mix_s[:, :, :],
                              b_rows[:, 0:D].rearrange("p (h i) -> p h i", h=KT)[:, :, 0:1].to_broadcast((128, KT, NS)), ADD) \
                .then_inc(mix_s_ready, 1)
            dve.wait_ge(mix_s_ready, 1)

            def op_rest(m, before):
                dve.wait_ge(op_hi_done, before + m + 1)
                dve.tensor_tensor(flat2(op_lo, m), prod[:, 0:TOK], flat2(op_hi, m).bitcast(f32), SUB).then_inc(op_lo_done, 1)

            def u_product(m):
                smp, prm = slice(0, NS), slice(NS, TOK)
                dve.wait_ge(mixed, START + m + 1)
                dve.wait_ge(op_lo_done, START + m)
                dve.tensor_tensor(prod[:, prm].rearrange("p (n d) -> p n d", n=8), bank_pair(6), over_tokens(b_rows, m), ADD) \
                    .then_inc(mix_biased, 1)
                dve.wait_ge(u_gelu, m + 1)
                dve.wait_ge(mix_biased, m + 1)
                dve.tensor_tensor(prod[:, smp], act_out[:, smp], flat2(mix_s, m), MUL)
                dve.tensor_tensor(prod[:, prm], prod[:, prm], act_out[:, prm], MUL).then_inc(u_prod, 1)
                op_rest(m, 0)

            with dve.Fori(0, KT - 1) as m:
                u_product(m)
                head(m + 1)
            u_product(KT - 1)

            with dve.Fori(0, KT) as m:
                dve.wait_ge(acc_full, FREE + R_A + 2 * m + 2)
                dve.wait_ge(a_sig, START + m + 1)
                dve.tensor_tensor(flat3(g, m), group(0), chunks(act_out[:, 0:TOK]), MUL).then_inc(a_out, 1)

            link(dve.memset(c_in[:, 0:2], 0.0))
            with dve.Fori(0, KT // 2) as i:
                for n in range(2):
                    m = 2 * i + n
                    x_grp, b_grp = (3 * n + 1) % 2, (3 * n + 2) % 2
                    xg, p0 = group(1 - x_grp), slice(NS, CW)
                    dve.wait_ge(acc_full, FREE + R_C + 6 * i + 3 * n + 2)
                    dve.wait_ge(c_copied, m + 1)
                    dve.tensor_tensor(tail[:, 2:2 + NS, ds(m, 1)].rearrange("p j a -> p (j a)"), xg[:, 0, 0:NS], act_out[:, 0:NS], MUL)
                    dve.tensor_tensor(c_in[:, 2:2 + CW - NS], xg[:, 0, p0], act_out[:, p0], MUL)
                    dve.tensor_tensor(c_in[:, 2 + CW - NS:2 + SEQ].rearrange("p (c w) -> p c w", c=2), xg[:, 1:3, :],
                                      act_out[:, CW:TOK].rearrange("p (c w) -> p c w", c=2), MUL).then_inc(cx_done, 1)
                    dve.wait_ge(cx_done, START + m + 1)
                    dve.wait_ge(op_hi_done, KT + m)
                    dve.tensor_copy(tail[:, 0:2, ds(m, 1)].rearrange("p j a -> p (j a)"), c_in[:, SEQ:SEQ + 2])
                    smp = (hist[:, ds(m, 1), 0, :], hist[:, ds(m, 1), 1, :], tail[:, 2:2 + NS, ds(m, 1)].rearrange("p j a -> p a j"))
                    out_s = prod[:, 0:NS].unsqueeze(1)
                    for k in range(3):
                        tap = par[:, ds(P_CONV + KT * k + m, 1)]
                        if k:
                            dve.wait_ge(conv_step, 2 * m + k)
                            dve.scalar_tensor_tensor(out_s, smp[k], tap, out_s, MUL, ADD)
                            ins = dve.scalar_tensor_tensor(prod[:, NS:TOK], c_in[:, k:k + SEQ], tap, prod[:, NS:TOK], MUL, ADD)
                        else:
                            dve.tensor_scalar(out_s, smp[k], tap, None, MUL)
                            ins = dve.tensor_scalar(prod[:, NS:TOK], c_in[:, k:k + SEQ], tap, None, MUL)
                        if k < 2:
                            ins.then_inc(conv_step, 1)
                    ins.then_inc(h_conv, 1)
                    dve.wait_ge(h_conv, m + 1)
                    dve.wait_ge(acc_full, FREE + R_C + 6 * i + 3 * n + 3)
                    dve.tensor_tensor(chunks(prod[:, 0:TOK]), group(1 - b_grp), chunks(prod[:, 0:TOK]), MUL).then_inc(c_prod, 1)
                    op_rest(m, KT)

            def b_combine(m):
                dve.wait_ge(acc_full, FREE + R_B + 2 * m + 2)
                dve.wait_ge(b_sig, START + m + 1)
                dve.wait_ge(h_sum, START + m)
                dve.tensor_tensor(chunks(prod[:, 0:TOK]), group(0), chunks(act_out[:, 0:TOK]), MUL).then_inc(b_out, 1)
                dve.wait_ge(b_out, START + m + 1)
                dve.tensor_tensor(flat2(g, m), flat2(g, m), prod[:, 0:TOK], ADD).then_inc(h_sum, 1)

            def h_rest(m):
                dve.wait_ge(h_hi, m + 1)
                dve.tensor_tensor(xn_lo[:, m, :], g[:, m, :], xn_hi[:, m, :].bitcast(f32), SUB).then_inc(h_lo, 1)

            dve.wait_ge(op_lo_done, START + 2 * KT)
            with dve.Fori(0, KT - 1) as m:
                b_combine(m)
            for m in range(KT - 1):
                h_rest(m)
            m = KT - 1
            dve.wait_ge(acc_full, FREE + R_O)
            dve.wait_ge(b_sig, START + KT)
            dve.wait_ge(h_sum, START + m)
            for c in range(CH):
                t = slice(CW * c, CW * c + CW)
                dve.tensor_tensor(prod[:, t], ps[:, c, 0:CW], act_out[:, t], MUL).then_inc(b_out, 1)
                dve.wait_ge(b_out, START + KT + c)
                dve.tensor_tensor(g[:, m, t], g[:, m, t], prod[:, t], ADD).then_inc(h_sum, 1)
            for c in range(CH):
                t = slice(CW * c, CW * c + CW)
                dve.wait_ge(h_hi, KT + c)
                dve.tensor_tensor(xn_lo[:, m, t], g[:, m, t], xn_hi[:, m, t].bitcast(f32), SUB).then_inc(h_lo, 1)

            base_t, root, inv, work = (tmp[5][:, 0:CW], tmp[5][:, CW:2 * CW], tmp[5][:, 2 * CW:3 * CW], tmp[6][:, 0:CW])

            def o_rsqrt(n, c):
                dve.wait_ge(n_sum, 2 * c + n + 1)
                dve.tensor_scalar(base_t, ps[:, 6 + n, 0:CW], 1.0 / D, EPS, MUL, ADD).then_inc(n_base, 1)
                dve.wait_ge(n_sqrt, 2 * c + n + 1)
                link(dve.reciprocal(inv, root))
                link(dve.tensor_tensor(work, inv, inv, MUL))
                link(dve.scalar_tensor_tensor(work, work, -0.5, base_t, MUL, MUL))
                link(dve.scalar_tensor_tensor(inv, work, 1.5, inv, ADD, MUL))

            def o_norm(c):
                t = slice(CW * c, CW * c + CW)
                gc, xc = g[:, :, t], xt[:, :, t]
                gains = par[:, P_PRE:P_PRE + KT].unsqueeze(2).to_broadcast((128, KT, CW))
                halves = [slice(0, KT // 2), slice(KT // 2, KT)]
                inv_half = inv.unsqueeze(1).to_broadcast((128, KT // 2, CW))
                o_rsqrt(0, c)
                dve.wait_ge(xt_in, 16)
                yield
                for h in halves:
                    link(dve.tensor_tensor(g[:, h, t], g[:, h, t], inv_half, MUL))
                    dve.tensor_tensor(xt[:, h, t], xt[:, h, t], g[:, h, t], ADD).then_inc(x1_done, 1)
                    yield
                yield
                dve.wait_ge(x1_sq, 2 * c + 2)
                dve.tensor_reduce(x1_sum, gc.rearrange("p m n -> p n m"), mybir.AxisListType.X, ADD).then_inc(x1_total, 1)
                yield
                o_rsqrt(1, c)
                yield
                for n, h in enumerate(halves):
                    for m in range(h.start, h.stop):
                        ins = dve.scalar_tensor_tensor(g[:, m, t], xt[:, m, t], par[:, P_PRE + m:P_PRE + m + 1], inv, MUL, MUL)
                    ins.then_inc(x1n_ready, 1)
                    yield
                for n, h in enumerate(halves):
                    dve.wait_ge(x1n_hi, 2 * c + n + 1)
                    ins = dve.tensor_tensor(xn_lo[:, h, t], g[:, h, t], xn_hi[:, h, t].bitcast(f32), SUB)
                ins.then_inc(x1n_lo, 1)
                yield

            dve.wait_ge(vs_out, 16)
            steps = iter(())
            for c in range(CH):
                for m in range(KT):
                    n = KT * c + m
                    dve.wait_ge(o_copied, n + 1)
                    if m == 0:
                        if c:
                            dve.wait_ge(n_sum, 2 * c - 1)
                        dve.tensor_copy(o_sum, o_square[n % 2]).then_inc(o_acc, 1)
                    else:
                        dve.wait_ge(o_acc, n)
                        dve.tensor_tensor(o_sum, o_sum, o_square[n % 2], ADD).then_inc(o_acc, 1)
                    next(steps, None)
                for _ in steps:
                    pass
                steps = o_norm(c)

            for counted in (f_prod, hid_lo):
                dve.sem_inc(counted, 2)

            def first_product(n):
                t = slice(CW * (n % 3), CW * (n % 3) + CW)
                dve.wait_ge(acc_full, FREE + R_F + 2 * n + 2)
                dve.wait_ge(p0_silu, n + 1)
                if n >= 3:
                    dve.wait_ge(p0_lo, n - 2)
                dve.tensor_tensor(prod[:, t], ps[:, (2 * n + 1) % 6, 0:CW], act_out[:, t], MUL).then_inc(p0_prod, 1)

            def first_rest(n):
                t = slice(CW * (n // 2), CW * (n // 2) + CW)
                dve.wait_ge(p0_hi, n + 1)
                dve.tensor_tensor(hid[:, 4 + n % 2, t], prod[:, CW * (n % 3):CW * (n % 3) + CW], hid[:, n % 2, t].bitcast(f32), SUB) \
                    .then_inc(p0_lo, 1)

            next(steps)
            next(steps)
            first_product(0)
            next(steps)
            first_rest(0)
            next(steps)
            first_product(1)
            next(steps)
            first_rest(1)
            for _ in steps:
                pass
            for n in range(2, 6):
                first_product(n)
                first_rest(n)
            link(dve.memset(g[:, :, :], 0.0))

            def hidden(j, i):
                dve.wait_ge(hid_lo, 2 * j + i)
                dve.tensor_tensor(chunks(prod[:, 0:TOK]), group(1), chunks(act_out[:, 0:TOK]), MUL).then_inc(f_prod, 1)
                dve.wait_ge(f_prod, 2 * j + i + 1)
                dve.wait_ge(hid_hi, 2 * j + i + 1)
                at = (j % 2) * 2 + i
                dve.tensor_tensor(flat2(hid, at + 4), prod[:, 0:TOK], flat2(hid, at).bitcast(f32), SUB).then_inc(hid_lo, 1)

            with dve.Fori(1, PAIRS) as j:
                for i in range(2):
                    dve.wait_ge(acc_full, pair(j) + 2 * i + 2)
                    dve.wait_ge(f_silu, 2 * j + i + 1)
                    hidden(j, i)
                for m in range(KT):
                    dve.wait_ge(acc_full, pair(j) + 4 + m + 1)
                    dve.wait_ge(f_acc, START + 8 * j - 7)
                    dst = g[:, m, :].rearrange("p (c w) -> p c w", c=CH)
                    dve.tensor_tensor(dst, dst, group(m % 2), ADD).then_inc(f_acc, 1)

            dve.tensor_tensor(gain_diag, ident[:, :].unsqueeze(1).to_broadcast((128, KT, 128)),
                              par[:, P_OUT:P_OUT + KT].unsqueeze(2).to_broadcast((128, KT, 128)), MUL).then_inc(diag_ready, 1)

            def finish(y):
                rows, _ = tokens(Y_TILES[y])
                a, r, w = (small[0:rows, 44 + n:45 + n] for n in range(3))
                dve.wait_ge(y_summed, y + 1)
                dve.tensor_scalar(a, ps[0:rows, 3, y:y + 1], 1.0 / D, EPS, MUL, ADD).then_inc(y_mean, 1)
                dve.wait_ge(y_mean, y + 1)
                rsqrt(r, a, w)
                dve.wait_ge(y_turned, y + 1)
                dve.wait_ge(x1_rows_done, y + 1)
                if y >= 3:
                    dve.wait_ge(y_out[y % 3], 16 * (y // 3))
                b = y_banks(y)
                dve.scalar_tensor_tensor(y_rows[y % 3][0:rows, 0:D].rearrange("p (a n) -> p a n", a=2), ps[0:rows, b:b + 2, :], r,
                                         token_source(y)[0:rows].rearrange("p (a n) -> p a n", a=2), MUL, ADD).then_inc(y_ready, 1)

            for q in range(CH * KT):
                c, m = divmod(q, KT)
                t = slice(CW * c, CW * c + CW)
                dve.wait_ge(acc_full, pair(PAIRS) + q + 1)
                dve.tensor_tensor(g[:, m, t], g[:, m, t], ps[:, q % 3, 0:CW], ADD).then_inc(y_acc, 1)
                if q >= 12 and q % 8 in (0, 4, 6):
                    finish((q - 12) // 8 * 3 + (q % 8 in (6,)) + 2 * (q % 8 == 0))
            for y in range(5, 9):
                finish(y)


_INS = ["x_prompt", "x_sample", "state_conv", "mix_pre_g", "mix_post_g", "w_in", "sgu_ln_g", "sgu_ln_b", "w_s", "b_s",
        "conv_w", "w_a_out", "w_b_out", "w_o", "ffn_pre_g", "ffn_post_g", "w_gate", "w_up", "w_down"]
_OUTS = [("y_prompt", (1, SEQ, D)), ("y_sample", (NS, 1, D)), ("conv_prompt", (1, 1, 2, D)),
         ("conv_sample", (1, NS, 2, D)), ("v_sample", (1, NS, 1, D))]


def kernel(**inputs):
    import concourse.bacc as bacc
    from concourse.bass_utils import run_bass_kernel_spmd as run

    nc = bacc.Bacc("TRN2", target_bir_lowering=False, num_devices=1, dynamic_dma_scratch_size=1024)
    arrays, args = {}, {}
    for name in _INS:
        a = np.ascontiguousarray(inputs[name])
        arrays["in_" + name] = a
        args[name] = nc.dram_tensor("in_" + name, a.shape, mybir.dt.from_np(a.dtype), kind="ExternalInput").ap()
    for name, shape in _OUTS:
        args[name] = nc.dram_tensor("out_" + name, shape, mybir.dt.float32, kind="ExternalOutput").ap()
    build(nc, **args)
    r = run(nc, [arrays], core_ids=[0])
    return tuple(r.results[0]["out_" + name] for name, _ in _OUTS)
```

```python
from contextlib import ExitStack

import numpy as np

import concourse.bass as bass
from concourse import mybir

D = 1024
SEQ = 1024
NS = 8
TOK = NS + SEQ
KT = D // 128
CH = 3
CW = TOK // CH
FFN = 2816
EPS = 1e-6
PAIRS = FFN // 256
COL_U, COL_V, COL_B, COL_C, COL_X, COL_RA, COL_RB = (i * D for i in range(7))

R_U = 0
R_A = R_U + KT
R_C = R_A + 2 * KT
R_B = R_C + 3 * KT
R_O = R_B + 2 * KT
R_F = R_O + KT
R_LOOP = R_F + 4
R_END = R_F + 6 * PAIRS
FREE = 9
A_O = FREE + R_O + CH - 1
A_F = A_O + CH * KT

START = 1

P_POST, P_PRE, P_OUT, P_CONV, P_ROWS = 0, KT, 2 * KT, 3 * KT, 6 * KT

O_SLOT = [2, 0, 1, 3, 4, 5, 6, 7] + [0, 1, 2, 3]
O_STAGE = [0, 1, 2, 3] * 2 + [0, 1] * 2
H_POOL = (0, 2, 3)
PARTS = [slice(0, 3), slice(3, 6), slice(6, 8)]
TMP_BYTES = ((TOK + 2) * 4 + 31) // 32 * 32
Y_TILES = [8, 0, 1, 2, 3, 4, 5, 6, 7]
PIECES = [(0, 3), (3, 5), (5, 7), (7, 9)]
Y_STEPS = {m: () for m in range(8)} | {2: (0,), 3: ("sum",), 4: (1,)}


def build(nc, x_prompt, x_sample, state_conv, mix_pre_g, mix_post_g, w_in, sgu_ln_g, sgu_ln_b, w_s,
          b_s, conv_w, w_a_out, w_b_out, w_o, ffn_pre_g, ffn_post_g, w_gate, w_up, w_down,
          y_prompt, y_sample, conv_prompt, conv_sample, v_sample):
    f32, f32r, i32 = mybir.dt.float32, mybir.dt.float32r, mybir.dt.int32
    ALU, ACT = mybir.AluOpType, mybir.ActivationFunctionType
    MUL, ADD, SUB = ALU.mult, ALU.add, ALU.subtract
    ds = bass.ds

    xt_dram = nc.dram_tensor("xt_dram", [128, KT, TOK], f32, kind="Internal").ap()

    ctx = ExitStack()
    with ctx:
        def sb(name, shape, dt=f32):
            return ctx.enter_context(nc.sbuf_tensor(name, shape, dt))

        def sem(name):
            return ctx.enter_context(nc.semaphore(name))

        tile_bytes = KT * TOK * 4
        op_at = (nc.sbuf_usable_end - 2 * tile_bytes) // 32 * 32
        xn_at = op_at - 2 * tile_bytes
        xn_hi = nc.alloc_sbuf_tensor_at("xn_hi", [128, KT, TOK], f32r, offset=xn_at)
        xn_lo = nc.alloc_sbuf_tensor_at("xn_lo", [128, KT, TOK], f32r, offset=xn_at + tile_bytes)
        y_raw = nc.alloc_sbuf_tensor_at("y_raw", [128, KT, TOK], f32, offset=xn_at)
        x1_rows = nc.alloc_sbuf_tensor_at("x1_rows", [128, 8, D], f32, offset=xn_at + tile_bytes)
        op_hi = nc.alloc_sbuf_tensor_at("op_hi", [128, KT, TOK], f32r, offset=op_at)
        op_lo = nc.alloc_sbuf_tensor_at("op_lo", [128, KT, TOK], f32r, offset=op_at + tile_bytes)
        xt = nc.alloc_sbuf_tensor_at("xt", [128, KT, TOK], f32, offset=op_at)
        hid = op_lo
        g = sb("g", [128, KT, TOK])
        gv = g[:, :, 0:D]
        stage = [sb(f"stage{i}", [128, D]) for i in range(2)]
        ring_hi = [sb(f"ring_hi{i}", [128, D], f32r) for i in range(2)]
        ring_lo = [sb(f"ring_lo{i}", [128, D], f32r) for i in range(2)]
        wide = {i: xn_at - (n + 1) * TMP_BYTES for n, i in enumerate((0, 1, 2, 7))}
        tmp = [nc.alloc_sbuf_tensor_at(f"tmp{i}", [128, TOK + 2], f32, offset=wide[i]) if i in wide else sb(f"tmp{i}", [128, TOK + 2])
               for i in range(8)]
        wide_r = {i: nc.alloc_sbuf_tensor_at(f"wide{i}", [128, D], f32r, offset=at) for i, at in wide.items()}
        ident = sb("ident", [128, 128])
        ones = sb("ones", [128, 128])
        par_rows = sb("par_rows", [P_ROWS, 128])
        par = sb("par", [128, P_ROWS])
        hist = sb("hist", [128, KT, 2, NS])
        ws00 = sb("ws00", [128, KT])
        mix_s = sb("mix_s", [128, KT, NS])
        tail = sb("tail", [128, 2 + NS, KT])
        tail_out = sb("tail_out", [(2 + NS) * KT, 128])
        small = sb("small", [128, 64])
        assert nc.sbuf_base <= min(wide.values()), (nc.sbuf_base, min(wide.values()))
        eps = small[:, 60:61]
        warm = small[:, 61:62]
        ps = ctx.enter_context(nc.psum_tensor("ps", [128, 8, 512], f32))

        x_rows = [tmp[0], tmp[1]]
        x_norm, x_save, pre_gain, v_smp, ws_t, ws_rows = tmp[2:8]
        hist_rows = tmp[5]
        act_out, v_head, prod, ln_g, ln_b = tmp[0:5]
        b_rows = tmp[7]
        c_in = tmp[1]
        o_stage = [stage[0], stage[1], tmp[4], tmp[6]]
        o_ring = [(ring_hi[n][:, :], ring_lo[n][:, :]) for n in range(2)] \
            + [(wide_r[1][:, :], wide_r[7][:, :])] \
            + [(op_lo[:, k, 0:D], op_lo[:, k + 1, 0:D]) for k in (2, 6, 0, 4)] \
            + [(wide_r[0][:, :], wide_r[2][:, :])]
        o_sum, o_square = tmp[3][:, 0:CW], [tmp[3][:, CW:2 * CW], tmp[3][:, 2 * CW:3 * CW]]
        x1_sum = tmp[4][:, 0:CW]
        base_t, root, inv, work = (tmp[5][:, 0:CW], tmp[5][:, CW:2 * CW], tmp[5][:, 2 * CW:3 * CW], tmp[6][:, 0:CW])
        y_square, y_sum = [tmp[3][:, 340 * n:340 * n + 340] for n in range(3)], tmp[4]
        y_rows = [tmp[5], tmp[6], tmp[7]]

        def group(i):
            return ps[:, 3 * i:3 * i + 3, 0:CW]

        def chunks(ap):
            return ap.rearrange("p (c w) -> p c w", c=CH)

        def flat2(t, m):
            return t[:, ds(m, 1), :].rearrange("p a n -> p (a n)")

        def flat3(t, m):
            return t[:, ds(m, 1), :].rearrange("p a (c w) -> p (a c) w", c=CH)

        def bank_pair(b, n=128):
            return ps[:, b:b + 2, :].rearrange("p a (k c) -> p (a k) c", c=128)[:, :, 0:n]

        def tokens(t):
            return (128, NS + 128 * t) if t < 8 else (NS, 0)

        consts = sem("consts")
        x_in = [sem("x_in0"), sem("x_in1")]
        wv_in = [sem(f"wv_in{k}") for k in range(KT)]
        wv_hi, wv_lo = sem("wv_hi"), sem("wv_lo")
        pre_in, ws_in, row_in, ws00_in = sem("pre_in"), sem("ws_in"), sem("row_in"), sem("ws00_in")
        ws_masked = sem("ws_masked")
        sumsq, x_scaled = sem("sumsq"), sem("x_scaled")
        raw_turned, norm_turned = sem("raw_turned"), sem("norm_turned")
        raw_copied, xt_saved = sem("raw_copied"), sem("xt_saved")
        xn_hi_done, xn_lo_done = sem("xn_hi_done"), sem("xn_lo_done")
        v_gelu, v_norm = sem("v_gelu"), sem("v_norm")
        chain = sem("chain")
        const_turned, ws_copied, par_copied = sem("const_turned"), sem("ws_copied"), sem("par_copied")
        ln_g_in, ln_b_in, b_in = sem("ln_g_in"), sem("ln_b_in"), sem("b_in")
        vs_ready, vs_turned, vs_out, mix_s_ready = sem("vs_ready"), sem("vs_turned"), sem("vs_out"), sem("mix_s_ready")
        w_in_done = [sem("w_loaded0"), sem("w_loaded1")]
        w_hi, pool_hi, w_lo = sem("w_hi"), sem("pool_hi"), sem("w_lo")
        acc_full = sem("acc_full")
        u_gelu, head_scaled, head_ready = sem("u_gelu"), sem("head_scaled"), sem("head_ready")
        mixed, mix_biased, u_prod = sem("mixed"), sem("mix_biased"), sem("u_prod")
        op_hi_done, op_lo_done = sem("op_hi_done"), sem("op_lo_done")
        a_sig, a_out = sem("a_sig"), sem("a_out")
        c_copied, cx_done, conv_step, h_conv, c_prod = sem("c_copied"), sem("cx_done"), sem("conv_step"), sem("h_conv"), sem("c_prod")
        tail_turned, tail_copied, tail_saved, hist_saved = sem("tail_turned"), sem("tail_copied"), sem("tail_saved"), sem("hist_saved")
        b_sig, b_out, h_sum = sem("b_sig"), sem("b_out"), sem("h_sum")
        h_hi, h_hi_last, h_lo = sem("h_hi"), sem("h_hi_last"), sem("h_lo")
        xt_in = [sem(f"xt_in{c}") for c in range(CH)]
        o_copied, o_acc = sem("o_copied"), sem("o_acc")
        n_sum, n_sqrt, n_base = sem("n_sum"), sem("n_sqrt"), sem("n_base")
        x1_done, x1_sq, x1_total, x1n_ready, x1n_hi, x1n_lo = sem("x1_done"), sem("x1_sq"), sem("x1_total"), sem("x1n_ready"), sem("x1n_hi"), sem("x1n_lo")
        f_silu, f_prod, hid_hi, hid_lo, f_acc = sem("f_silu"), sem("f_prod"), sem("hid_hi"), sem("hid_lo"), sem("f_acc")
        o_in = [sem(f"o_in{n}") for n in range(4)]
        inv_ready, x1_pool = sem("inv_ready"), sem("x1_pool")
        h_lo_pool, x1n_lo_pool = sem("h_lo_pool"), sem("x1n_lo_pool")
        p0_silu, p0_prod, p0_hi, p0_lo = sem("p0_silu"), sem("p0_prod"), sem("p0_hi"), sem("p0_lo")
        y_root = sem("y_root")
        y_gained, y_added = sem("y_gained"), sem("y_added")
        x1_turned, x1_rows_done = sem("x1_turned"), sem("x1_rows_done")
        y_acc, y_squared, y_mean = sem("y_acc"), sem("y_squared"), sem("y_mean")
        y_summed, y_turned, y_ready = sem("y_summed"), sem("y_turned"), sem("y_ready")
        y_out = [sem(f"y_out{n}") for n in range(3)]

        def pair(j):
            return 12 * j + A_F

        def token_source(y):
            t = Y_TILES[y]
            return x1_rows[:, t, :] if t < 8 else tmp[1][:, 0:D]

        def y_banks(y):
            return 4 + 2 * (y % 2)

        def scale_of(c, n):
            return small[:, 12 * c + 3 * n:12 * c + 3 * n + PIECES[c][1] - PIECES[c][0]]

        def piece(c):
            first, last = (Y_TILES[i] for i in (PIECES[c][0], PIECES[c][1] - 1))
            return slice(tokens(first)[1], tokens(last)[1] + 128)

        block = ctx.enter_context(nc.Block())

        @block.sync
        def _(sp):
            def x_load(t):
                rows, _ = tokens(t)
                if t >= 2:
                    sp.wait_ge(raw_turned, t - 1)
                    sp.wait_ge(x_scaled, t - 1)
                src = x_prompt[0, 128 * t:128 * t + 128, :] if t < 8 else x_sample[:, 0, :]
                sp.dma_start(x_rows[t % 2][0:rows, 0:D], src).then_inc(x_in[t % 2], 16)

            def wv_load(k):
                sp.dma_start(gv[:, k, :], w_in[0, 128 * k:128 * k + 128, COL_V:COL_V + D]).then_inc(wv_in[k], 16)

            def load(slot, src):
                sp.dma_start(stage[slot][:, :].rearrange("p (k c) -> p k c", k=src.shape[1]), src) \
                    .then_inc(w_in_done[slot], 16)

            def columns(w, at):
                return w.rearrange("(k p) n -> p k n", p=128)[:, :, ds(at, 128)]

            def down(j, half):
                return w_down[0].rearrange("(j k p) n -> p j k n", p=128, k=2)[:, ds(j, 1), :, 512 * half:512 * half + 512] \
                    .rearrange("p a k n -> p (a k) n")

            x_load(0)
            sp.dma_start(pre_gain[:, 0:D], mix_pre_g[0:1, :].to_broadcast((128, D))).then_inc(pre_in, 16)
            wv_load(0)
            wv_load(1)
            wv_load(2)
            x_load(1)
            for k in range(3, 6):
                wv_load(k)
            x_load(2)
            for k in range(6, KT):
                wv_load(k)
            load(0, columns(w_in[0], COL_U))
            load(1, columns(w_in[0], COL_U + 128))
            for t in range(3, 9):
                x_load(t)
            sp.wait_ge(x_scaled, 9)
            sp.dma_start(ln_b[:, 0:D], sgu_ln_b[0:1, :].to_broadcast((128, D))).then_inc(ln_b_in, 16)
            sp.wait_ge(xt_saved, 16 * 9)
            sp.dma_start(ln_g[:, 0:D], sgu_ln_g[0:1, :].to_broadcast((128, D))).then_inc(ln_g_in, 16)
            sp.wait_ge(const_turned, 1)
            sp.dma_start(b_rows[:, 0:D], b_s[0:1].rearrange("a h i -> a (h i)").to_broadcast((128, D))).then_inc(b_in, 16)

            for m in range(2, KT):
                sp.wait_ge(w_lo, R_U + m - 1)
                load(m % 2, columns(w_in[0], COL_U + m * 128))
            with sp.Fori(1, KT + 1) as n:
                for s, (w, c0) in enumerate(((w_in[0], COL_RA), (w_a_out[0], 0))):
                    sp.wait_ge(w_lo, R_A + 2 * n - 2 + s - 1)
                    load(s, columns(w, n * 128 + c0 - 128))
            with sp.Fori(0, KT // 2) as i:
                for n in range(6):
                    at = sp.snap((COL_C, COL_X, COL_B)[n % 3] + n // 3 * 128 + i * 256)
                    sp.wait_ge(w_lo, R_C + 6 * i + n - 1)
                    load(n % 2, columns(w_in[0], at))
            with sp.Fori(1, KT + 1) as n:
                for s, (w, c0) in enumerate(((w_in[0], COL_RB), (w_b_out[0], 0))):
                    sp.wait_ge(w_lo, R_B + 2 * n - 2 + s - 1)
                    load(s, columns(w, n * 128 + c0 - 128))
            sp.wait_ge(op_lo_done, START + 2 * KT)
            for n in range(KT + 4):
                b = O_STAGE[n]
                before = [i for i in range(n) if O_STAGE[i] == b]
                if before:
                    sp.wait_ge(w_lo, R_O + before[-1] + 1)
                elif b < 2:
                    sp.wait_ge(w_lo, R_O - 2 + b + 1)
                src = columns(w_o[0], n * 128) if n < KT else columns((w_gate, w_up)[n % 2][0], (n - KT) // 2 * 128)
                sp.dma_start(o_stage[b][:, 0:D].rearrange("p (k c) -> p k c", k=KT), src).then_inc(o_in[b], 16)
                if n == KT - 1:
                    sp.wait_ge(acc_full, A_O)
                    for c in range(CH):
                        sp.dma_start(xt[:, :, CW * c:CW * c + CW], xt_dram[:, :, CW * c:CW * c + CW]).then_inc(xt_in[c], 16)
            for n in range(4):
                sp.wait_ge(w_lo, R_LOOP + n - 1)
                load(n % 2, columns((w_gate, w_up)[n % 2][0], 256 + n // 2 * 128))
            with sp.Fori(1, PAIRS - 1) as j:
                for n in range(2):
                    before = sp.snap(j - 1)
                    sp.wait_ge(w_lo, R_LOOP + 6 * j - 2 + n - 1)
                    load(n, down(before, n))
                for n in range(4):
                    at = sp.snap(j * 256 + 256 + n // 2 * 128)
                    sp.wait_ge(w_lo, R_LOOP + 6 * j + n - 1)
                    load(n % 2, columns((w_gate, w_up)[n % 2][0], at))
            for n in range(4):
                sp.wait_ge(w_lo, R_LOOP + 6 * (PAIRS - 1) - 2 + n - 1)
                load(n % 2, down(PAIRS - 2 + n // 2, n % 2))

            for y, t in enumerate(Y_TILES):
                rows, _ = tokens(t)
                sp.wait_ge(y_ready, y + 1)
                dst = y_prompt[0, 128 * t:128 * t + 128, :] if t < 8 else y_sample[:, 0, :]
                sp.dma_start(dst, y_rows[y % 3][0:rows, 0:D]).then_inc(y_out[y % 3], 16)
            for n in range(3):
                sp.wait_ge(y_out[n], 16 * 3)
            sp.wait_ge(vs_out, 16)
            sp.wait_ge(hist_saved, 16)
            sp.wait_ge(tail_saved, 16 * (1 + NS))
            sp.wait_ge(xt_saved, 16 * 9)

        @block.gpsimd
        def _(pool):
            pool.memset(ident[:, :], 0.0).then_inc(consts, 1)
            pool.memset(ones[:, :], 1.0).then_inc(consts, 1)
            pool.memset(eps, EPS).then_inc(consts, 1)
            pool.wait_ge(consts, 3)
            pool.affine_select(out=ident[:, :], in_=ident[:, :], compare_op=ALU.not_equal, fill=1.0, base=0,
                               pattern=[[-1, 128]], channel_multiplier=1).then_inc(consts, 1)
            pool.wait_ge(ws_in, 16)
            wsv = ws_rows[:, 0:D].rearrange("p (h j) -> p h j", h=KT)
            pool.affine_select(out=wsv, in_=wsv, compare_op=ALU.is_ge, fill=0.0, base=0,
                               pattern=[[0, KT], [-1, 128]], channel_multiplier=1).then_inc(ws_masked, 1)

            def rest(src, hi, lo):
                pool.tensor_tensor(lo, src, hi.bitcast(f32), SUB).then_inc(w_lo, 1)

            for r in range(2):
                pool.wait_ge(w_in_done[r], 16)
                pool.tensor_copy(ring_hi[r][:, :], stage[r][:, :]).then_inc(pool_hi, 1)
                pool.wait_ge(pool_hi, r + 1)
                rest(stage[r][:, :], ring_hi[r][:, :], ring_lo[r][:, :])
            with pool.Fori(1, R_O // 2) as i:
                for s in range(2):
                    pool.wait_ge(w_hi, 2 * i + s - 1)
                    rest(stage[s][:, :], ring_hi[s][:, :], ring_lo[s][:, :])

            def o_rest(n):
                pool.wait_ge(w_hi, R_O + n - 1)
                rest(o_stage[O_STAGE[n]][:, 0:D], *o_ring[O_SLOT[n]])

            def x1n_rest(c, parts):
                t = slice(CW * c, CW * c + CW)
                for n, h in enumerate(PARTS[:parts]):
                    pool.wait_ge(x1n_hi, len(PARTS) * c + n + 1)
                    pool.tensor_tensor(xn_lo[:, h, t], g[:, h, t], xn_hi[:, h, t].bitcast(f32), SUB).then_inc(x1n_lo_pool, 1)

            def x1_part(c):
                t, h = slice(CW * c, CW * c + CW), PARTS[-1]
                pool.wait_ge(inv_ready, c + 1)
                pool.wait_ge(xt_in[c], 16)
                pool.tensor_tensor(g[:, h, t], g[:, h, t], inv.unsqueeze(1).to_broadcast((128, h.stop - h.start, CW)), MUL) \
                    .then_inc(x1_pool, 1)
                pool.wait_ge(x1_pool, 2 * c + 1)
                pool.tensor_tensor(xt[:, h, t], xt[:, h, t], g[:, h, t], ADD).then_inc(x1_pool, 1)

            o_rest(0)
            for m in H_POOL:
                pool.wait_ge(h_hi, m + 1)
                pool.tensor_tensor(xn_lo[:, m, :], g[:, m, :], xn_hi[:, m, :].bitcast(f32), SUB).then_inc(h_lo_pool, 1)
            for n in range(1, KT):
                o_rest(n)

            def add_square(c, m):
                n = (KT - 1) * c + m - 1
                pool.wait_ge(o_copied, KT * c + m + 1)
                if m > 1:
                    pool.wait_ge(o_acc, n)
                pool.tensor_tensor(o_sum, o_sum, o_square[n % 2], ADD).then_inc(o_acc, 1)

            for c in range(CH):
                for m in range(1, KT):
                    add_square(c, m)
                    if c and m == 1:
                        x1_part(c - 1)
                    if c == CH - 1 and m >= 4:
                        o_rest(KT + m - 4)
                if c == 1:
                    x1n_rest(0, len(PARTS))
            x1_part(CH - 1)
            x1n_rest(CH - 1, 1)
            with pool.Fori(R_LOOP // 2, R_END // 2) as i:
                for s in range(2):
                    pool.wait_ge(w_hi, 2 * i + s - 1)
                    rest(stage[s][:, :], ring_hi[s][:, :], ring_lo[s][:, :])

            for c in range(len(PIECES)):
                t = piece(c)
                for m in range(1, KT):
                    n = (KT - 1) * c + m - 1
                    pool.wait_ge(y_squared, KT * c + m + 1)
                    if m > 1:
                        pool.wait_ge(y_added, n)
                    pool.tensor_tensor(y_sum[:, t], y_sum[:, t], y_square[n % 3][:, 0:t.stop - t.start], ADD).then_inc(y_added, 1)

        @block.tensor
        def _(pe):
            def three(out, w_h, w_l, x_h, x_l, first, last):
                ins = None
                for n, (w, x) in enumerate(((w_h, x_h), (w_h, x_l), (w_l, x_h))):
                    for o, xc in zip(out, x):
                        ins = pe.matmul(o, w, xc, start=first and n == 0, stop=last and n == 2)
                return ins

            def parts(x, k, n=CH):
                return [x[:, k, CW * c:CW * c + CW] for c in range(n)]

            def unit(slot, grp, x_h, x_l):
                out = [ps[:, 3 * grp + c, 0:CW] for c in range(CH)]
                for k in range(KT):
                    w = slice(128 * k, 128 * k + 128)
                    ins = three(out, ring_hi[slot][:, w], ring_lo[slot][:, w], parts(x_h, k), parts(x_l, k), k == 0, k == KT - 1)
                ins.then_inc(acc_full, 1)

            def turn_raw(t):
                rows, _ = tokens(t)
                pe.wait_ge(x_in[t % 2], 16 * (t // 2 + 1))
                if t:
                    pe.wait_ge(raw_copied, t)
                for k in range(KT):
                    ins = pe.transpose(ps[:, 4 + k // 4, 128 * (k % 4):128 * (k % 4) + rows],
                                       x_rows[t % 2][0:rows, 128 * k:128 * k + 128], ident[0:rows, 0:rows])
                ins.then_inc(raw_turned, 1)

            def turn_norm(t):
                rows, _ = tokens(t)
                pe.wait_ge(x_scaled, t + 1)
                if t:
                    pe.wait_ge(xn_lo_done, t)
                for k in range(KT):
                    ins = pe.transpose(ps[:, 6 + k // 4, 128 * (k % 4):128 * (k % 4) + rows],
                                       x_norm[0:rows, 128 * k:128 * k + 128], ident[0:rows, 0:rows])
                ins.then_inc(norm_turned, 1)

            def v_tile(t):
                _, at = tokens(t)
                pe.wait_ge(xn_lo_done, t + 1)
                if t >= 2:
                    pe.wait_ge(v_gelu, t - 1)
                out = [ps[:, 2 * (t % 2) + n, :] for n in range(2)]
                for k in range(KT):
                    if t == 0:
                        if k == 3:
                            turn_norm(1)
                        pe.wait_ge(wv_lo, k + 1)
                    w_h, w_l = ([w[:, k, 512 * n:512 * n + 512] for n in range(2)] for w in (op_hi, op_lo))
                    ins = three(out, xn_hi[:, k, at:at + 128], xn_lo[:, k, at:at + 128], w_h, w_l, k == 0, k == KT - 1)
                ins.then_inc(acc_full, 1)

            pe.sem_inc(mixed, START)
            pe.wait_ge(consts, 4)
            turn_raw(0)
            turn_norm(0)
            turn_raw(1)
            for t in range(9):
                v_tile(t)
                if t + 2 < 9:
                    turn_raw(t + 2)
                    turn_norm(t + 2)
                if t == 7:
                    pe.wait_ge(raw_copied, 9)
                    pe.wait_ge(xn_lo_done, 9)
                    pe.wait_ge(row_in, 16 * 6)
                    pe.wait_ge(ws_masked, 1)
                    pe.transpose(ps[:, 4, 0:P_ROWS], par_rows[:, :], ident[0:P_ROWS, 0:P_ROWS])
                    for k in range(KT):
                        pe.transpose(ps[:, 4, 128 + 16 * k:144 + 16 * k], hist_rows[0:2 * NS, 128 * k:128 * k + 128],
                                     ident[0:2 * NS, 0:2 * NS])
                    for h in range(KT):
                        ins = pe.transpose(ps[:, 6 + h // 4, 128 * (h % 4):128 * (h % 4) + 128],
                                           ws_rows[:, 128 * h:128 * h + 128], ident[:, :])
                    ins.then_inc(const_turned, 1)
            pe.wait_ge(v_gelu, 8)
            pe.wait_ge(par_copied, 1)

            def mix(m):
                pe.wait_ge(head_ready, m + 1)
                pe.wait_ge(mix_biased, m)
                for n in range(8):
                    ins = pe.matmul(ps[:, 6 + n // 4, 128 * (n % 4):128 * (n % 4) + 128],
                                    v_head[:, 128 * n:128 * n + 128], ws_t[:, ds(m * 128, 128)], start=True, stop=True)
                ins.then_inc(mixed, 1)

            pe.wait_ge(w_lo, 1)
            unit(0, 1, xn_hi, xn_lo)
            pe.wait_ge(vs_ready, 1)
            pe.wait_ge(v_gelu, 9)
            for k in range(KT):
                ins = pe.transpose(ps[:, 0, NS * k:NS * k + NS], v_smp[0:NS, 128 * k:128 * k + 128], ident[0:NS, 0:NS])
            ins.then_inc(vs_turned, 1)
            pe.wait_ge(ws_copied, 1)
            mix(0)
            pe.wait_ge(w_lo, 2)
            pe.wait_ge(mix_s_ready, 1)
            unit(1, 0, xn_hi, xn_lo)
            mix(1)
            with nc.Fori(1, KT // 2, engines=[mybir.EngineType.PE], hint_back_edge=True) as i:
                for s in range(2):
                    m = 2 * i + s
                    pe.wait_ge(w_lo, R_U + m + 1)
                    pe.wait_ge(u_gelu, m - 1)
                    unit(s, 1 - s, xn_hi, xn_lo)
                    mix(m)

            pe.wait_ge(u_gelu, KT)
            with nc.Fori(0, KT, engines=[mybir.EngineType.PE], hint_back_edge=True) as m:
                pe.wait_ge(w_lo, R_A + 2 * m + 1)
                pe.wait_ge(a_sig, START + m)
                unit(0, 1, xn_hi, xn_lo)
                pe.wait_ge(w_lo, R_A + 2 * m + 2)
                pe.wait_ge(a_out, START + m)
                pe.wait_ge(op_lo_done, START + KT)
                unit(1, 0, op_hi, op_lo)

            with nc.Fori(0, KT // 2, engines=[mybir.EngineType.PE], hint_back_edge=True) as i:
                for n in range(6):
                    m = 2 * i + n // 3
                    pe.wait_ge(w_lo, R_C + 6 * i + n + 1)
                    if n % 3 == 0:
                        pe.wait_ge(cx_done, START + m)
                        if n == 0:
                            pe.wait_ge(a_sig, START + KT)
                    elif n % 3 == 1:
                        pe.wait_ge(c_prod, START + m)
                        if n == 1:
                            pe.wait_ge(a_out, START + KT)
                    else:
                        pe.wait_ge(c_copied, m + 1)
                    unit(n % 2, 1 - n % 2, xn_hi, xn_lo)

            pe.wait_ge(h_conv, KT)
            pe.transpose(ps[0:(2 + NS) * KT, 6, 0:128], tail[:, :, :].rearrange("p j m -> p (j m)"), ident[:, :]) \
                .then_inc(tail_turned, 1)
            def r_b(m):
                pe.wait_ge(w_lo, R_B + 2 * m + 1)
                pe.wait_ge(b_sig, START + m)
                unit(0, 1, xn_hi, xn_lo)

            with nc.Fori(0, KT - 1, engines=[mybir.EngineType.PE], hint_back_edge=True) as m:
                r_b(m)
                pe.wait_ge(w_lo, R_B + 2 * m + 2)
                pe.wait_ge(b_out, START + m)
                pe.wait_ge(op_lo_done, START + 2 * KT)
                unit(1, 0, op_hi, op_lo)

            def chunk_unit(w_h, w_l, x_h, x_l, c, bank, within=None):
                t = slice(CW * c, CW * c + CW)
                for k in range(KT):
                    if within and k == within[0]:
                        within[1](within[2])
                    w = slice(128 * k, 128 * k + 128)
                    ins = three([ps[:, bank, 0:CW]], w_h[:, w], w_l[:, w], [x_h[:, k, t]], [x_l[:, k, t]], k == 0, k == KT - 1)
                ins.then_inc(acc_full, 1)

            r_b(KT - 1)
            pe.wait_ge(w_lo, R_O)
            pe.wait_ge(b_out, START + KT - 1)
            for c in range(CH):
                chunk_unit(ring_hi[1], ring_lo[1], op_hi, op_lo, c, c)

            def norm_sum(n, at):
                pe.matmul(ps[:, 6 + n % 2, 0:CW], ones[:, :], at, start=True, stop=True).then_inc(n_sum, 1)

            def first_norm(c):
                pe.wait_ge(o_acc, (KT - 1) * (c + 1))
                norm_sum(0, tmp[3][:, 0:CW])

            def second_norm(c):
                pe.wait_ge(x1_total, c + 1)
                norm_sum(1, tmp[4][:, 0:CW])

            pe.wait_ge(b_out, START + KT)
            pe.wait_ge(tail_copied, 1)

            pe.wait_ge(h_lo_pool, len(H_POOL))
            for c in range(CH):
                pe.wait_ge(h_lo, KT - 1 - len(H_POOL) + c + 1)
                for m in range(KT):
                    n = KT * c + m
                    pe.wait_ge(w_lo, R_O + m + 1)
                    if n in (1, 2):
                        pe.wait_ge(b_out, START + KT + n)
                    if n >= 6:
                        pe.wait_ge(o_copied, n - 5)
                    chunk_unit(*o_ring[O_SLOT[m]], xn_hi, xn_lo, c, n % 6, {0: (6, first_norm, c - 1), 5: (1, second_norm, c - 1)}.get(m) if c else None)

            for c in range(CH):
                if c == 0:
                    pe.wait_ge(x1n_lo_pool, len(PARTS))
                else:
                    pe.wait_ge(x1n_lo, c)
                if c == CH - 1:
                    pe.wait_ge(x1n_lo_pool, len(PARTS) + 1)
                for f in range(4):
                    n = 4 * c + f
                    pe.wait_ge(w_lo, R_F + f + 1)
                    if n < 6:
                        pe.wait_ge(o_copied, CH * KT - 5 + n)
                    else:
                        pe.wait_ge((p0_silu, p0_prod)[n % 2], (n - 6) // 2 + 1)
                    chunk_unit(*o_ring[O_SLOT[KT + f]], xn_hi, xn_lo, c, n % 6, {0: (6, first_norm, CH - 1), 5: (1, second_norm, CH - 1)}.get(n))

            def down(j, behind=None):
                pe.wait_ge(p0_lo, 6)
                pe.wait_ge(hid_lo, 2 * j)
                for m in range(KT):
                    slot = m // 4
                    if m % 4 == 0:
                        pe.wait_ge(w_lo, R_LOOP + 6 * (j - 1) + 4 + slot + 1)
                    if m < 2:
                        pe.wait_ge((f_silu, f_prod)[m], 2 * j + 2)
                    else:
                        pe.wait_ge(f_acc, START + 8 * j - 8 + m)
                    for k in range(2):
                        w = slice(512 * k + 128 * (m % 4), 512 * k + 128 * (m % 4) + 128)
                        at = ((j - 1) % 2) * 2 + k
                        x_h, x_l = ([hid[:, ds(o + at, 1), CW * c:CW * c + CW].rearrange("p a n -> p (a n)") for c in range(CH)]
                                    for o in (0, 4))
                        ins = three([ps[:, 3 * (m % 2) + c, 0:CW] for c in range(CH)],
                                    ring_hi[slot][:, w], ring_lo[slot][:, w], x_h, x_l, k == 0, k == 1)
                    ins.then_inc(acc_full, 1)
                    if behind:
                        behind(m)

            def gate_up(j):
                for n in range(4):
                    pe.wait_ge(w_lo, R_LOOP + 6 * (j - 1) + n + 1)
                    if n < 2:
                        pe.wait_ge(p0_silu, 5 + n)
                        if n:
                            pe.wait_ge(p0_prod, 6)
                        pe.wait_ge(f_acc, START + 8 * j - 8 + n)
                    pe.wait_ge((f_silu, f_prod)[n % 2], 2 * j + n // 2)
                    unit(n % 2, n % 2, xn_hi, xn_lo)

            def turn_x1(y):
                rows, at = tokens(Y_TILES[y])
                if y:
                    pe.wait_ge(x1_rows_done, y)
                for k in range(KT):
                    ins = pe.transpose(ps[0:rows, 6 + k // 4, 128 * (k % 4):128 * (k % 4) + 128], xt[:, k, at:at + rows], ident[:, :])
                ins.then_inc(x1_turned, 1)

            with nc.Fori(1, PAIRS - 1, engines=[mybir.EngineType.PE], hint_back_edge=True) as j:
                gate_up(j)
                down(j)
            gate_up(PAIRS - 1)
            down(PAIRS - 1, behind=turn_x1)

            def sum_piece(c):
                pe.wait_ge(y_added, (KT - 1) * (c + 1))
                if c:
                    pe.wait_ge(y_mean, c)
                for y in range(*PIECES[c]):
                    _, at = tokens(Y_TILES[y])
                    ins = pe.matmul(ps[:, 3, y:y + 1], y_sum[:, at:at + 128], ones[:, 0:1], start=True, stop=True)
                ins.then_inc(y_summed, 1)

            def turn_y(y):
                rows, at = tokens(Y_TILES[y])
                c = [y < last for _, last in PIECES].index(True)
                pe.wait_ge(y_gained, KT * (c + 1))
                if y == 1:
                    pe.wait_ge(x1_rows_done, 9)
                elif y:
                    pe.wait_ge(y_ready, y - 1)
                b = y_banks(y)
                for k in range(KT):
                    ins = pe.transpose(ps[0:rows, b + k // 4, 128 * (k % 4):128 * (k % 4) + 128], g[:, k, at:at + rows], ident[:, :])
                ins.then_inc(y_turned, 1)

            pe.wait_ge(w_lo, R_END - 1)
            pe.wait_ge(hid_lo, 2 * PAIRS)
            pe.wait_ge(f_acc, START + 8 * (PAIRS - 1))
            for q in range(len(PIECES) * KT):
                c, m = divmod(q, KT)
                if q == KT // 2:
                    pe.wait_ge(w_lo, R_END)
                if q >= 3:
                    pe.wait_ge(y_acc, q - 2)
                t = piece(c)
                for k in range(2):
                    w = slice(512 * k + 128 * (m % 4), 512 * k + 128 * (m % 4) + 128)
                    at = (PAIRS - 1) % 2 * 2 + k
                    ins = three([ps[:, q % 3, 0:t.stop - t.start]], ring_hi[m // 4][:, w], ring_lo[m // 4][:, w],
                                [hid[:, at, t]], [hid[:, at + 4, t]], k == 0, k == 1)
                ins.then_inc(acc_full, 1)
                if q == 0:
                    turn_x1(8)
                for step in Y_STEPS[m] if c else []:
                    if step == "sum":
                        sum_piece(c - 1)
                    else:
                        turn_y(PIECES[c - 1][0] + step)
                if q == 2 * KT:
                    turn_y(2)
            turn_y(7)
            sum_piece(len(PIECES) - 1)
            turn_y(8)

        @block.scalar
        def _(act):
            for counted in (a_sig, b_sig):
                act.sem_inc(counted, START)
            act.wait_ge(consts, 3)
            act.activation(warm, eps, ACT.Gelu_apprx_tanh)

            def square(t):
                rows, _ = tokens(t)
                act.wait_ge(x_in[t % 2], 16 * (t // 2 + 1))
                if t:
                    act.wait_ge(norm_turned, t)
                act.activation(x_norm[0:rows, 0:D], x_rows[t % 2][0:rows, 0:D], ACT.Square,
                               accum_out=small[0:rows, t:t + 1]).then_inc(sumsq, 1)

            def wv_split(k):
                act.wait_ge(wv_in[k], 16)
                act.activation(op_hi[:, k, 0:D], gv[:, k, :], ACT.Copy).then_inc(wv_hi, 1)

            def norm_split(t):
                rows, at = tokens(t)
                act.wait_ge(norm_turned, t + 1)
                act.activation(xn_hi[:, :, at:at + rows], bank_pair(6, rows), ACT.Copy).then_inc(xn_hi_done, 1)

            def keep(t):
                rows, at = tokens(t)
                if t == 1:
                    norm_split(t)
                    square(2)
                act.wait_ge(raw_turned, t + 1)
                if t:
                    act.wait_ge(xt_saved, 16 * t)
                saved = x_save[:, 0:KT * rows].rearrange("p (k n) -> p k n", k=KT)
                act.activation(saved, bank_pair(4, rows), ACT.Copy).then_inc(raw_copied, 1)
                if t != 1:
                    norm_split(t)
                act.wait_ge(raw_copied, t + 1)
                act.dma_start(xt_dram[:, :, at:at + rows], saved).then_inc(xt_saved, 16)

            square(0)
            wv_split(0)
            wv_split(1)
            keep(0)
            wv_split(2)
            square(1)
            for k in range(3, KT):
                wv_split(k)
            keep(1)
            for t in range(9):
                if 0 < t < 7:
                    square(t + 2)
                if t == 0:
                    for n, src in enumerate((mix_post_g, ffn_pre_g, ffn_post_g)):
                        act.dma_start(par_rows[KT * n:KT * n + KT, :], src[0].rearrange("(k p) -> k p", p=128)).then_inc(row_in, 16)
                if t == 1:
                    act.dma_start(ws_rows[:, 0:D].rearrange("p (h j) -> p h j", h=KT), w_s[0].rearrange("h i j -> i h j")).then_inc(ws_in, 16)
                    act.dma_start(par_rows[P_CONV:P_ROWS, :], conv_w[0].rearrange("w (k p) -> (w k) p", p=128)).then_inc(row_in, 16)
                if t == 2:
                    for n in range(2):
                        act.dma_start(hist_rows[NS * n:NS * n + NS, 0:D], state_conv[0, :, n, :]).then_inc(row_in, 16)
                if t == 3:
                    with nc.allow_non_contiguous_dma(reason="8 scalars to each partition"):
                        act.dma_start(ws00[:, :], w_s[0, :, 0, 0:1].rearrange("h a -> a h").to_broadcast((128, KT))).then_inc(ws00_in, 16)
                    act.dma_start(conv_sample[0, :, 0, :], state_conv[0, :, 1, :]).then_inc(hist_saved, 16)
                act.wait_ge(acc_full, t + 1)
                rows, _ = tokens(t)
                if t < 8:
                    if t == 0:
                        act.wait_ge(wv_lo, KT)
                    dst = gv[:, t, :]
                else:
                    act.wait_ge(const_turned, 1)
                    dst = v_smp[0:NS, 0:D]
                act.activation(dst.rearrange("p (a n) -> p a n", a=2), ps[0:rows, 2 * (t % 2):2 * (t % 2) + 2, :],
                               ACT.Gelu_apprx_tanh).then_inc(v_gelu, 1)
                if t + 2 < 9:
                    keep(t + 2)
            act.wait_ge(const_turned, 1)
            act.activation(ws_t[:, 0:D].rearrange("p (k n) -> p k n", k=KT), bank_pair(6), ACT.Copy).then_inc(ws_copied, 1)

            def ring_split(s, loads):
                act.wait_ge(w_in_done[s], 16 * loads)
                act.activation(ring_hi[s][:, :], stage[s][:, :], ACT.Copy).then_inc(w_hi, 1)

            def op_split(m, n):
                act.activation(flat2(op_hi, m), prod[:, 0:TOK], ACT.Copy).then_inc(op_hi_done, 1)

            with act.Fori(0, KT // 2) as i:
                for s in range(2):
                    m = 2 * i + s
                    act.wait_ge(acc_full, FREE + R_U + m + 1)
                    act.wait_ge(u_prod, START + m)
                    act.activation(chunks(act_out[:, 0:TOK]), group(1 - s), ACT.Gelu_apprx_tanh).then_inc(u_gelu, 1)
                    ring_split(s, R_U // 2 + i + 2)
                    act.wait_ge(u_prod, START + m + 1)
                    op_split(m, 0)
            act.wait_ge(vs_ready, 1)
            act.dma_start(v_sample[0, :, 0, :], v_smp[0:NS, 0:D]).then_inc(vs_out, 16)

            act.activation(warm, eps, ACT.Sigmoid)
            with act.Fori(0, KT) as m:
                act.wait_ge(acc_full, FREE + R_A + 2 * m + 1)
                act.wait_ge(a_out, START + m)
                act.activation(chunks(act_out[:, 0:TOK]), group(1), ACT.Sigmoid).then_inc(a_sig, 1)
                ring_split(0, R_A // 2 + m + 2)
                act.wait_ge(acc_full, FREE + R_A + 2 * m + 2)
                ring_split(1, R_A // 2 + m + 2)

            act.wait_ge(a_out, START + KT)
            with act.Fori(0, KT // 2) as i:
                for n in range(2):
                    m = 2 * i + n
                    act.wait_ge(acc_full, FREE + R_C + 6 * i + 3 * n + 1)
                    act.wait_ge(cx_done, START + m)
                    act.activation(chunks(act_out[:, 0:TOK]), group(1 - n), ACT.Copy).then_inc(c_copied, 1)
                    for u in range(3):
                        at = 3 * n + u
                        if u:
                            act.wait_ge(acc_full, FREE + R_C + 6 * i + at + 1)
                        ring_split(at % 2, R_C // 2 + 3 * i + at // 2 + 2)
                    act.wait_ge(c_prod, START + m + 1)
                    op_split(m, KT)

            act.wait_ge(tail_turned, 1)
            act.activation(tail_out[:, :], ps[0:(2 + NS) * KT, 6, 0:128], ACT.Copy).then_inc(tail_copied, 1)
            act.wait_ge(tail_copied, 1)
            act.dma_start(conv_prompt[0, 0].rearrange("t (k p) -> (t k) p", p=128), tail_out[0:2 * KT, :]).then_inc(tail_saved, 16)
            for b in range(NS):
                act.dma_start(conv_sample[0, b, 1, :].rearrange("(k p) -> k p", p=128),
                              tail_out[KT * (2 + b):KT * (3 + b), :]).then_inc(tail_saved, 16)
            act.activation(warm, eps, ACT.Sigmoid)

            def b_gate(m):
                act.wait_ge(acc_full, FREE + R_B + 2 * m + 1)
                act.wait_ge(b_out, START + m)
                act.activation(chunks(act_out[:, 0:TOK]), group(1), ACT.Sigmoid).then_inc(b_sig, 1)

            with act.Fori(0, KT - 1) as m:
                b_gate(m)
                ring_split(0, R_B // 2 + m + 2)
                act.wait_ge(acc_full, FREE + R_B + 2 * m + 2)
                ring_split(1, R_B // 2 + m + 2)

            def o_split(n):
                b = O_STAGE[n]
                act.wait_ge(o_in[b], 16 * sum(O_STAGE[i] == b for i in range(n + 1)))
                act.activation(o_ring[O_SLOT[n]][0], o_stage[b][:, 0:D], ACT.Copy).then_inc(w_hi, 1)

            def h_split(m):
                act.wait_ge(h_sum, START + m + 1)
                act.activation(xn_hi[:, m, :], g[:, m, :], ACT.Copy).then_inc(h_hi, 1)

            def h_last(c):
                t = slice(CW * c, CW * c + CW)
                act.wait_ge(h_sum, START + KT + c)
                act.activation(xn_hi[:, KT - 1, t], g[:, KT - 1, t], ACT.Copy).then_inc(h_hi_last, 1)

            o_split(0)
            b_gate(KT - 1)
            for m in range(KT - 1):
                h_split(m)
            for c in range(CH):
                h_last(c)
                if c == 1:
                    act.wait_ge(acc_full, A_O)
                o_split(c + 1)
            for n in range(CH + 1, KT):
                o_split(n)

            def sqrt(n, c):
                act.wait_ge(n_base, 2 * c + n + 1)
                act.activation(tmp[5][:, CW:2 * CW], tmp[5][:, 0:CW], ACT.Sqrt).then_inc(n_sqrt, 1)

            def x1_squares(c):
                t = slice(CW * c, CW * c + CW)
                for n, h in enumerate(PARTS):
                    if h is PARTS[-1]:
                        act.wait_ge(x1_pool, 2 * c + 2)
                    else:
                        act.wait_ge(x1_done, (len(PARTS) - 1) * c + n + 1)
                    act.activation(g[:, h, t], xt[:, h, t], ACT.Square).then_inc(x1_sq, 1)

            def x1n_split(c):
                t = slice(CW * c, CW * c + CW)
                for n, h in enumerate(PARTS):
                    act.wait_ge(x1n_ready, len(PARTS) * c + n + 1)
                    act.activation(xn_hi[:, h, t], g[:, h, t], ACT.Copy).then_inc(x1n_hi, 1)

            act.activation(warm, eps, ACT.Sqrt)
            for c in range(CH):
                for m in range(KT):
                    n = KT * c + m
                    act.wait_ge(acc_full, A_O + n + 1)
                    act.activation(g[:, m, CW * c:CW * c + CW], ps[:, n % 6, 0:CW], ACT.Copy, scale=par[:, P_POST + m:P_POST + m + 1])
                    added = (KT - 1) * c + m - 1
                    if m and added >= 2:
                        act.wait_ge(o_acc, added - 1)
                    if m == 0 and c:
                        act.wait_ge(n_sum, 2 * c - 1)
                    act.activation(o_square[added % 2] if m else o_sum, ps[:, n % 6, 0:CW], ACT.Square).then_inc(o_copied, 1)
                    if c and m == 0:
                        sqrt(0, c - 1)
                    if c and m == 2:
                        x1_squares(c - 1)
                    if c and m == 4:
                        sqrt(1, c - 1)
                    if c and m == (6 if c == CH - 1 else 7):
                        x1n_split(c - 1)
                    if c == CH - 1 and m in (1, 2, 5, 7):
                        o_split(KT + (1, 2, 5, 7).index(m))


            def gate(j, i):
                act.activation(chunks(act_out[:, 0:TOK]), group(0), ACT.Silu).then_inc(f_silu, 1)

            def hidden(j, i):
                act.wait_ge(f_prod, 2 * j + i + 1)
                act.activation(flat2(hid, (j % 2) * 2 + i), prod[:, 0:TOK], ACT.Copy).then_inc(hid_hi, 1)

            def first_gate(n):
                act.wait_ge(acc_full, A_F + 2 * n + 1)
                if n >= 3:
                    act.wait_ge(p0_prod, n - 2)
                act.activation(act_out[:, CW * (n % 3):CW * (n % 3) + CW], ps[:, 2 * n % 6, 0:CW], ACT.Silu).then_inc(p0_silu, 1)

            def first_hidden(n):
                t = slice(CW * (n // 2), CW * (n // 2) + CW)
                act.wait_ge(p0_prod, n + 1)
                act.activation(hid[:, n % 2, t], prod[:, CW * (n % 3):CW * (n % 3) + CW], ACT.Copy).then_inc(p0_hi, 1)

            sqrt(0, CH - 1)
            first_gate(0)
            x1_squares(CH - 1)
            first_hidden(0)
            first_gate(1)
            first_hidden(1)
            x1n_split(CH - 1)
            for n in range(2, 6):
                first_gate(n)
                if n >= 4:
                    act.wait_ge(acc_full, A_F + 9 + n - 4)
                    ring_split(n - 4, R_O // 2 + 1)
                first_hidden(n)
            for counted in (f_silu, hid_hi):
                act.sem_inc(counted, 2)
            def act_pair(j, behind=None):
                for i in range(2):
                    act.wait_ge(acc_full, pair(j) + 2 * i + 1)
                    act.wait_ge(f_prod, 2 * j + i)
                    gate(j, i)
                    ring_split(0, R_O // 2 - 3 + 3 * j + i + 2)
                    act.wait_ge(acc_full, pair(j) + 2 * i + 2)
                    ring_split(1, R_O // 2 - 3 + 3 * j + i + 2)
                    hidden(j, i)
                for half in range(2):
                    for m in range(4 * half, 4 * half + 4) if behind else []:
                        behind(m)
                    act.wait_ge(acc_full, pair(j) + 8 + 4 * half)
                    ring_split(half, R_O // 2 - 3 + 3 * j + 4)

            def keep_x1(y):
                rows, _ = tokens(Y_TILES[y])
                act.wait_ge(x1_turned, y + 1)
                act.activation(token_source(y)[0:rows].rearrange("p (a n) -> p a n", a=2), ps[0:rows, 6:8, :], ACT.Copy) \
                    .then_inc(x1_rows_done, 1)

            with act.Fori(1, PAIRS - 1) as j:
                act_pair(j)
            act_pair(PAIRS - 1, behind=keep_x1)

            def y_sqrt(c):
                act.wait_ge(y_mean, c + 1)
                act.activation(scale_of(c, 1), scale_of(c, 0), ACT.Sqrt).then_inc(y_root, 1)

            for q in range(len(PIECES) * KT):
                c, m = divmod(q, KT)
                t = piece(c)
                n = (KT - 1) * c + m - 1
                act.wait_ge(y_acc, q + 1)
                if m and n >= 3:
                    act.wait_ge(y_added, n - 2)
                act.activation(y_square[n % 3][:, 0:t.stop - t.start] if m else y_sum[:, t], y_raw[:, m, t], ACT.Square).then_inc(y_squared, 1)
                act.activation(g[:, m, t], y_raw[:, m, t], ACT.Copy, scale=par[:, P_OUT + m:P_OUT + m + 1]).then_inc(y_gained, 1)
                if q == 0:
                    keep_x1(8)
                    act.activation(warm, eps, ACT.Sqrt)
                if c and m == 4:
                    y_sqrt(c - 1)
            y_sqrt(len(PIECES) - 1)

        @block.vector
        def _(dve):
            links = [0]

            def link(ins):
                links[0] += 1
                ins.then_inc(chain, 1)
                dve.wait_ge(chain, links[0])

            def rsqrt(y, a, t):
                link(dve.tensor_scalar(y.bitcast(i32), a.bitcast(i32), -0.5, float(0x5F3759DF), MUL, ADD))
                for _ in range(3):
                    link(dve.tensor_tensor(t, y, y, MUL))
                    link(dve.scalar_tensor_tensor(t, t, -0.5, a, MUL, MUL))
                    link(dve.scalar_tensor_tensor(y, t, 1.5, y, ADD, MUL))

            def scale_rows(t):
                rows, _ = tokens(t)
                a, y, w = (small[0:rows, 20 + n:21 + n] for n in range(3))
                dve.wait_ge(sumsq, t + 1)
                link(dve.tensor_scalar(a, small[0:rows, t:t + 1], 1.0 / D, EPS, MUL, ADD))
                rsqrt(y, a, w)
                dve.wait_ge(pre_in, 16)
                dve.scalar_tensor_tensor(x_norm[0:rows, 0:D], x_rows[t % 2][0:rows, 0:D], y,
                                         pre_gain[0:rows, 0:D], MUL, MUL).then_inc(x_scaled, 1)

            def wv_rest(k):
                dve.wait_ge(wv_hi, k + 1)
                dve.tensor_tensor(op_lo[:, k, 0:D], gv[:, k, :], op_hi[:, k, 0:D].bitcast(f32), SUB).then_inc(wv_lo, 1)

            def xn_rest(t):
                rows, at = tokens(t)
                dve.wait_ge(xn_hi_done, t + 1)
                dve.tensor_tensor(xn_lo[:, :, at:at + rows], bank_pair(6, rows),
                                  xn_hi[:, :, at:at + rows].bitcast(f32), SUB).then_inc(xn_lo_done, 1)

            def v_layer_norm(t):
                rows, _ = tokens(t)
                v = gv[:, t, :] if t < 8 else v_smp[0:NS, 0:D]
                dve.wait_ge(v_gelu, t + 1)
                dve.bn_stats(small[0:rows, 24:30], v[:, 0:512])
                link(dve.bn_stats(small[0:rows, 30:36], v[:, 512:1024]))
                link(dve.bn_aggr(small[0:rows, 36:38], small[0:rows, 24:36]))
                a, y, w = (small[0:rows, 40 + n:41 + n] for n in range(3))
                link(dve.tensor_scalar(a, small[0:rows, 37:38], EPS, None, ADD))
                rsqrt(y, a, w)
                dve.tensor_scalar(v, v, small[0:rows, 36:37], y, SUB, MUL).then_inc(v_norm, 1)

            for counted in (u_prod, op_lo_done, a_out, cx_done, c_prod, b_out, h_sum):
                dve.sem_inc(counted, START)
            dve.sem_inc(f_acc, START + 1)
            scale_rows(0)
            for k in range(2):
                wv_rest(k)
            xn_rest(0)
            wv_rest(2)
            scale_rows(1)
            for k in range(3, KT):
                wv_rest(k)
            xn_rest(1)
            for t in range(9):
                if t + 2 < 9:
                    scale_rows(t + 2)
                v_layer_norm(t)
                if t + 2 < 9:
                    xn_rest(t + 2)
                if t == 7:
                    dve.wait_ge(const_turned, 1)
                    dve.tensor_copy(par[:, :], ps[:, 4, 0:P_ROWS])
                    dve.tensor_copy(hist[:, :, :, :].rearrange("p k t b -> p (k t b)"), ps[:, 4, 128:256]).then_inc(par_copied, 1)
            dve.wait_ge(v_norm, 9)
            dve.wait_ge(ln_g_in, 16)
            dve.wait_ge(ln_b_in, 16)
            link(dve.tensor_tensor(v_smp[0:NS, 0:D], v_smp[0:NS, 0:D], ln_g[0:NS, 0:D], MUL))
            dve.tensor_tensor(v_smp[0:NS, 0:D], v_smp[0:NS, 0:D], ln_b[0:NS, 0:D], ADD).then_inc(vs_ready, 1)

            def over_tokens(row, m):
                return row[:, ds(m * 128, 128)].unsqueeze(1).to_broadcast((128, 8, 128))

            def head(m):
                dst = v_head[:, 0:D].rearrange("p (n d) -> p n d", n=8)
                dve.wait_ge(mixed, START + m)
                dve.tensor_tensor(dst, gv[:, :, ds(m * 128, 128)], over_tokens(ln_g, m), MUL).then_inc(head_scaled, 1)
                dve.wait_ge(head_scaled, m + 1)
                dve.tensor_tensor(dst, dst, over_tokens(ln_b, m), ADD).then_inc(head_ready, 1)

            head(0)
            dve.wait_ge(vs_turned, 1)
            dve.wait_ge(ws00_in, 16)
            dve.wait_ge(b_in, 16)
            link(dve.tensor_tensor(mix_s[:, :, :], ps[:, 0, 0:NS * KT].rearrange("p (k b) -> p k b", k=KT),
                                   ws00[:, :].unsqueeze(2).to_broadcast((128, KT, NS)), MUL))
            dve.tensor_tensor(mix_s[:, :, :], mix_s[:, :, :],
                              b_rows[:, 0:D].rearrange("p (h i) -> p h i", h=KT)[:, :, 0:1].to_broadcast((128, KT, NS)), ADD) \
                .then_inc(mix_s_ready, 1)
            dve.wait_ge(mix_s_ready, 1)

            def op_rest(m, before):
                dve.wait_ge(op_hi_done, before + m + 1)
                dve.tensor_tensor(flat2(op_lo, m), prod[:, 0:TOK], flat2(op_hi, m).bitcast(f32), SUB).then_inc(op_lo_done, 1)

            def u_product(m):
                smp, prm = slice(0, NS), slice(NS, TOK)
                dve.wait_ge(mixed, START + m + 1)
                dve.wait_ge(op_lo_done, START + m)
                dve.tensor_tensor(prod[:, prm].rearrange("p (n d) -> p n d", n=8), bank_pair(6), over_tokens(b_rows, m), ADD) \
                    .then_inc(mix_biased, 1)
                dve.wait_ge(u_gelu, m + 1)
                dve.wait_ge(mix_biased, m + 1)
                dve.tensor_tensor(prod[:, smp], act_out[:, smp], flat2(mix_s, m), MUL)
                dve.tensor_tensor(prod[:, prm], prod[:, prm], act_out[:, prm], MUL).then_inc(u_prod, 1)
                op_rest(m, 0)

            with dve.Fori(0, KT - 1) as m:
                u_product(m)
                head(m + 1)
            u_product(KT - 1)

            with dve.Fori(0, KT) as m:
                dve.wait_ge(acc_full, FREE + R_A + 2 * m + 2)
                dve.wait_ge(a_sig, START + m + 1)
                dve.tensor_tensor(flat3(g, m), group(0), chunks(act_out[:, 0:TOK]), MUL).then_inc(a_out, 1)

            link(dve.memset(c_in[:, 0:2], 0.0))
            with dve.Fori(0, KT // 2) as i:
                for n in range(2):
                    m = 2 * i + n
                    x_grp, b_grp = (3 * n + 1) % 2, (3 * n + 2) % 2
                    xg, p0 = group(1 - x_grp), slice(NS, CW)
                    dve.wait_ge(acc_full, FREE + R_C + 6 * i + 3 * n + 2)
                    dve.wait_ge(c_copied, m + 1)
                    dve.tensor_tensor(tail[:, 2:2 + NS, ds(m, 1)].rearrange("p j a -> p (j a)"), xg[:, 0, 0:NS], act_out[:, 0:NS], MUL)
                    dve.tensor_tensor(c_in[:, 2:2 + CW - NS], xg[:, 0, p0], act_out[:, p0], MUL)
                    dve.tensor_tensor(c_in[:, 2 + CW - NS:2 + SEQ].rearrange("p (c w) -> p c w", c=2), xg[:, 1:3, :],
                                      act_out[:, CW:TOK].rearrange("p (c w) -> p c w", c=2), MUL).then_inc(cx_done, 1)
                    dve.wait_ge(cx_done, START + m + 1)
                    dve.wait_ge(op_hi_done, KT + m)
                    dve.tensor_copy(tail[:, 0:2, ds(m, 1)].rearrange("p j a -> p (j a)"), c_in[:, SEQ:SEQ + 2])
                    smp = (hist[:, ds(m, 1), 0, :], hist[:, ds(m, 1), 1, :], tail[:, 2:2 + NS, ds(m, 1)].rearrange("p j a -> p a j"))
                    out_s = prod[:, 0:NS].unsqueeze(1)
                    for k in range(3):
                        tap = par[:, ds(P_CONV + KT * k + m, 1)]
                        if k:
                            dve.wait_ge(conv_step, 2 * m + k)
                            dve.scalar_tensor_tensor(out_s, smp[k], tap, out_s, MUL, ADD)
                            ins = dve.scalar_tensor_tensor(prod[:, NS:TOK], c_in[:, k:k + SEQ], tap, prod[:, NS:TOK], MUL, ADD)
                        else:
                            dve.tensor_scalar(out_s, smp[k], tap, None, MUL)
                            ins = dve.tensor_scalar(prod[:, NS:TOK], c_in[:, k:k + SEQ], tap, None, MUL)
                        if k < 2:
                            ins.then_inc(conv_step, 1)
                    ins.then_inc(h_conv, 1)
                    dve.wait_ge(h_conv, m + 1)
                    dve.wait_ge(acc_full, FREE + R_C + 6 * i + 3 * n + 3)
                    dve.tensor_tensor(chunks(prod[:, 0:TOK]), group(1 - b_grp), chunks(prod[:, 0:TOK]), MUL).then_inc(c_prod, 1)
                    op_rest(m, KT)

            def b_combine(m):
                dve.wait_ge(acc_full, FREE + R_B + 2 * m + 2)
                dve.wait_ge(b_sig, START + m + 1)
                dve.wait_ge(h_sum, START + m)
                dve.tensor_tensor(chunks(prod[:, 0:TOK]), group(0), chunks(act_out[:, 0:TOK]), MUL).then_inc(b_out, 1)
                dve.wait_ge(b_out, START + m + 1)
                dve.tensor_tensor(flat2(g, m), flat2(g, m), prod[:, 0:TOK], ADD).then_inc(h_sum, 1)

            def h_rest(m):
                dve.wait_ge(h_hi, m + 1)
                dve.tensor_tensor(xn_lo[:, m, :], g[:, m, :], xn_hi[:, m, :].bitcast(f32), SUB).then_inc(h_lo, 1)

            def h_last(c):
                t = slice(CW * c, CW * c + CW)
                dve.wait_ge(acc_full, FREE + R_O + c)
                dve.tensor_tensor(prod[:, t], ps[:, c, 0:CW], act_out[:, t], MUL).then_inc(b_out, 1)
                dve.wait_ge(b_out, START + KT + c)
                dve.tensor_tensor(g[:, KT - 1, t], g[:, KT - 1, t], prod[:, t], ADD).then_inc(h_sum, 1)

            dve.wait_ge(op_lo_done, START + 2 * KT)
            with dve.Fori(0, KT - 1) as m:
                b_combine(m)
            dve.wait_ge(b_sig, START + KT)
            dve.wait_ge(h_sum, START + KT - 1)
            def last_rest(c):
                t = slice(CW * c, CW * c + CW)
                dve.wait_ge(h_hi_last, c + 1)
                dve.tensor_tensor(xn_lo[:, KT - 1, t], g[:, KT - 1, t], xn_hi[:, KT - 1, t].bitcast(f32), SUB).then_inc(h_lo, 1)

            mine = [m for m in range(KT - 1) if m not in H_POOL]
            for m in mine:
                h_rest(m)
                if m == mine[1]:
                    h_last(0)
            last_rest(0)
            for c in range(1, CH):
                h_last(c)
                last_rest(c)

            def o_rsqrt(n, c):
                dve.wait_ge(n_sum, 2 * c + n + 1)
                if (n, c) == (1, CH - 1):
                    link(dve.tensor_scalar(base_t, ps[:, 6 + n, 0:CW], 1.0 / D, EPS, MUL, ADD))
                    rsqrt(inv, base_t, work)
                    return
                dve.tensor_scalar(base_t, ps[:, 6 + n, 0:CW], 1.0 / D, EPS, MUL, ADD).then_inc(n_base, 1)
                dve.wait_ge(n_sqrt, 2 * c + n + 1)
                link(dve.reciprocal(inv, root))
                link(dve.tensor_tensor(work, inv, inv, MUL))
                link(dve.scalar_tensor_tensor(work, work, -0.5, base_t, MUL, MUL))
                ins = dve.scalar_tensor_tensor(inv, work, 1.5, inv, ADD, MUL)
                if n == 0:
                    ins.then_inc(inv_ready, 1)
                    dve.wait_ge(inv_ready, c + 1)
                else:
                    link(ins)

            def x1(c):
                t = slice(CW * c, CW * c + CW)
                o_rsqrt(0, c)
                dve.wait_ge(xt_in[c], 16)
                for h in PARTS[:-1]:
                    link(dve.tensor_tensor(g[:, h, t], g[:, h, t], inv.unsqueeze(1).to_broadcast((128, h.stop - h.start, CW)), MUL))
                    dve.tensor_tensor(xt[:, h, t], xt[:, h, t], g[:, h, t], ADD).then_inc(x1_done, 1)

            def x1_squares_sum(c):
                dve.wait_ge(x1_sq, len(PARTS) * (c + 1))
                dve.tensor_reduce(x1_sum, g[:, :, CW * c:CW * c + CW].rearrange("p m n -> p n m"), mybir.AxisListType.X, ADD) \
                    .then_inc(x1_total, 1)

            def x1_norm(c):
                t = slice(CW * c, CW * c + CW)
                o_rsqrt(1, c)
                for h in PARTS:
                    for m in range(h.start, h.stop):
                        ins = dve.scalar_tensor_tensor(g[:, m, t], xt[:, m, t], par[:, P_PRE + m:P_PRE + m + 1], inv, MUL, MUL)
                    ins.then_inc(x1n_ready, 1)

            def x1n_rest(c, first):
                t = slice(CW * c, CW * c + CW)
                for n in range(first, len(PARTS)):
                    h = PARTS[n]
                    dve.wait_ge(x1n_hi, len(PARTS) * c + n + 1)
                    ins = dve.tensor_tensor(xn_lo[:, h, t], g[:, h, t], xn_hi[:, h, t].bitcast(f32), SUB)
                ins.then_inc(x1n_lo, 1)

            dve.wait_ge(vs_out, 16)
            for c in range(CH - 1):
                x1(c)
                x1_squares_sum(c)
                x1_norm(c)
                if c:
                    x1n_rest(c, 0)

            for counted in (f_prod, hid_lo):
                dve.sem_inc(counted, 2)

            def first_product(n):
                t = slice(CW * (n % 3), CW * (n % 3) + CW)
                dve.wait_ge(acc_full, A_F + 2 * n + 2)
                dve.wait_ge(p0_silu, n + 1)
                if n >= 3:
                    dve.wait_ge(p0_lo, n - 2)
                dve.tensor_tensor(prod[:, t], ps[:, (2 * n + 1) % 6, 0:CW], act_out[:, t], MUL).then_inc(p0_prod, 1)

            def first_rest(n):
                t = slice(CW * (n // 2), CW * (n // 2) + CW)
                dve.wait_ge(p0_hi, n + 1)
                dve.tensor_tensor(hid[:, 4 + n % 2, t], prod[:, CW * (n % 3):CW * (n % 3) + CW], hid[:, n % 2, t].bitcast(f32), SUB) \
                    .then_inc(p0_lo, 1)

            c = CH - 1
            x1(c)
            first_product(0)
            x1_squares_sum(c)
            first_rest(0)
            first_product(1)
            x1_norm(c)
            x1n_rest(c, 1)
            first_rest(1)
            for n in range(2, 6):
                first_product(n)
                first_rest(n)
            link(dve.memset(g[:, :, :], 0.0))

            def hidden(j, i):
                dve.wait_ge(hid_lo, 2 * j + i)
                dve.tensor_tensor(chunks(prod[:, 0:TOK]), group(1), chunks(act_out[:, 0:TOK]), MUL).then_inc(f_prod, 1)

            def hidden_rest(j, i):
                dve.wait_ge(f_prod, 2 * j + i + 1)
                dve.wait_ge(hid_hi, 2 * j + i + 1)
                at = (j % 2) * 2 + i
                dve.tensor_tensor(flat2(hid, at + 4), prod[:, 0:TOK], flat2(hid, at).bitcast(f32), SUB).then_inc(hid_lo, 1)

            with dve.Fori(1, PAIRS) as j:
                for i in range(2):
                    dve.wait_ge(acc_full, pair(j) + 2 * i + 2)
                    dve.wait_ge(f_silu, 2 * j + i + 1)
                    hidden(j, i)
                    if i == 0:
                        hidden_rest(j, 0)
                for m in range(KT):
                    if m == 1:
                        hidden_rest(j, 1)
                    dve.wait_ge(acc_full, pair(j) + 4 + m + 1)
                    dve.wait_ge(f_acc, START + 8 * j - 7)
                    dst = g[:, m, :].rearrange("p (c w) -> p c w", c=CH)
                    dve.tensor_tensor(dst, dst, group(m % 2), ADD).then_inc(f_acc, 1)

            def mean_square(c):
                first, last = PIECES[c]
                dve.wait_ge(y_summed, c + 1)
                dve.tensor_scalar(scale_of(c, 0), ps[:, 3, first:last], 1.0 / D, EPS, MUL, ADD).then_inc(y_mean, 1)

            def scales(c):
                a, root, r, w = (scale_of(c, n) for n in range(4))
                dve.wait_ge(y_root, c + 1)
                link(dve.reciprocal(r, root))
                link(dve.tensor_tensor(w, r, r, MUL))
                link(dve.scalar_tensor_tensor(w, w, -0.5, a, MUL, MUL))
                link(dve.scalar_tensor_tensor(r, w, 1.5, r, ADD, MUL))

            def finish(y, c):
                rows, _ = tokens(Y_TILES[y])
                at = y - PIECES[c][0]
                dve.wait_ge(y_turned, y + 1)
                dve.wait_ge(x1_rows_done, y + 1)
                if y >= 3:
                    dve.wait_ge(y_out[y % 3], 16 * (y // 3))
                b = y_banks(y)
                dve.scalar_tensor_tensor(y_rows[y % 3][0:rows, 0:D].rearrange("p (a n) -> p a n", a=2), ps[0:rows, b:b + 2, :],
                                         scale_of(c, 2)[0:rows, at:at + 1], token_source(y)[0:rows].rearrange("p (a n) -> p a n", a=2), MUL, ADD) \
                    .then_inc(y_ready, 1)

            for q in range(len(PIECES) * KT):
                c, m = divmod(q, KT)
                t = piece(c)
                dve.wait_ge(acc_full, pair(PAIRS) + q + 1)
                dve.tensor_tensor(y_raw[:, m, t], g[:, m, t], ps[:, q % 3, 0:t.stop - t.start], ADD).then_inc(y_acc, 1)
                if c and m == 4:
                    mean_square(c - 1)
                if c and m == 5:
                    scales(c - 1)
                if c and m >= 6:
                    finish(PIECES[c - 1][0] + m - 6, c - 1)
                if c == 2 and m == 1:
                    finish(2, 0)
            c = len(PIECES) - 1
            mean_square(c)
            scales(c)
            for y in range(*PIECES[c]):
                finish(y, c)


_INS = ["x_prompt", "x_sample", "state_conv", "mix_pre_g", "mix_post_g", "w_in", "sgu_ln_g", "sgu_ln_b", "w_s", "b_s",
        "conv_w", "w_a_out", "w_b_out", "w_o", "ffn_pre_g", "ffn_post_g", "w_gate", "w_up", "w_down"]
_OUTS = [("y_prompt", (1, SEQ, D)), ("y_sample", (NS, 1, D)), ("conv_prompt", (1, 1, 2, D)),
         ("conv_sample", (1, NS, 2, D)), ("v_sample", (1, NS, 1, D))]


def kernel(**inputs):
    import concourse.bacc as bacc
    from concourse.bass_utils import run_bass_kernel_spmd as run

    nc = bacc.Bacc("TRN2", target_bir_lowering=False, num_devices=1, dynamic_dma_scratch_size=1024)
    arrays, args = {}, {}
    for name in _INS:
        a = np.ascontiguousarray(inputs[name])
        arrays["in_" + name] = a
        args[name] = nc.dram_tensor("in_" + name, a.shape, mybir.dt.from_np(a.dtype), kind="ExternalInput").ap()
    for name, shape in _OUTS:
        args[name] = nc.dram_tensor("out_" + name, shape, mybir.dt.float32, kind="ExternalOutput").ap()
    build(nc, **args)
    r = run(nc, [arrays], core_ids=[0])
    return tuple(r.results[0]["out_" + name] for name, _ in _OUTS)
```
